# Optimizing a Trainium2 kernel written in Bass

```python
import math
import jax, jax.numpy as jnp
from jax import lax
import numpy as np

D_MODEL = 1024
BATCH = 1
SEQ = 256
DEPTH = 2

GRID_W = 64
CTX_LEN = 256
N_MIXERS = 2
N_SSD_LAYERS = (DEPTH + 1) // 2
N_ATTN_LAYERS = DEPTH // 2
EPS = 1e-6

SSD_EXPAND = 2
D_INNER = SSD_EXPAND * D_MODEL
SSD_HEAD_DIM = 64
SSD_HEADS = D_INNER // SSD_HEAD_DIM
SSD_GROUPS = 4
SSD_HEADS_PER_GROUP = SSD_HEADS // SSD_GROUPS
D_STATE = 128
CONV_W = 5
CHUNK = 128
D_CONV_CH = D_INNER + 2 * SSD_GROUPS * D_STATE
D_IN_PROJ = 2 * D_INNER + 2 * SSD_GROUPS * D_STATE + 2 * SSD_HEADS

DA_HEADS = D_MODEL // 128
DA_HEAD_DIM = 64
DA_V_DIM = 2 * DA_HEAD_DIM
DA_QKV = 3 * DA_HEADS * 2 * DA_HEAD_DIM
Q_BLOCK = 128
ROPE_THETA = 10000.0
ROPE_PAIRS_PER_AXIS = DA_HEAD_DIM // 4

D_FF = -(-8 * D_MODEL // (3 * 256)) * 256

kernel_name = "hybrid_ssd_diffattn_dit_prefix"

def rmsnorm(x, w):
    xf = x.astype(jnp.float32)
    y = xf * lax.rsqrt(jnp.mean(xf * xf, axis=-1, keepdims=True) + EPS)
    return (y * w.astype(jnp.float32)).astype(x.dtype)

def modulate(h, shift, scale):
    return h * (1 + scale) + shift

def swiglu(h, w_gate, w_up, w_down):
    return (jax.nn.silu(h @ w_gate) * (h @ w_up)) @ w_down

def dwconv_centred(u, w, b):
    y = lax.conv_general_dilated(
        u, w[:, None, :].astype(u.dtype), window_strides=(1,),
        padding=[(CONV_W // 2, CONV_W // 2)],
        dimension_numbers=("NWC", "WIO", "NWC"),
        feature_group_count=u.shape[-1])
    return y + b

def _segsum_exp(a_cum):
    n = a_cum.shape[-1]
    mask = jnp.tril(jnp.ones((n, n), dtype=bool))
    diff = a_cum[..., :, None] - a_cum[..., None, :]
    return jnp.exp(jnp.where(mask, diff, -jnp.inf))

def ssd_scan(x, dt, a, b, c, h0):
    bsz, L, H, P = x.shape
    G, N = b.shape[2], b.shape[3]
    Hg = H // G
    nc = L // CHUNK
    f32 = jnp.float32
    xd = (x.astype(f32) * dt[..., None]).reshape(bsz, nc, CHUNK, G, Hg, P)
    adt = (dt * a).reshape(bsz, nc, CHUNK, G, Hg).transpose(0, 3, 4, 1, 2)
    a_cum = jnp.cumsum(adt, axis=-1)
    bc = b.astype(f32).reshape(bsz, nc, CHUNK, G, N)
    cc = c.astype(f32).reshape(bsz, nc, CHUNK, G, N)
    cb = jnp.einsum('bclgn,bcsgn->bgcls', cc, bc)
    wmat = cb[:, :, None] * _segsum_exp(a_cum)
    y_diag = jnp.einsum('bghcls,bcsghp->bclghp', wmat, xd)
    decay_states = jnp.exp(a_cum[..., -1:] - a_cum).transpose(0, 3, 4, 1, 2)
    states = jnp.einsum('bclgn,bclghp->cbghpn', bc, xd * decay_states[..., None])
    chunk_decay = jnp.exp(a_cum[..., -1]).transpose(3, 0, 1, 2)

    def step(h, inp):
        s_c, d_c = inp
        return h * d_c[..., None, None] + s_c, h

    h_last, h_prev = lax.scan(step, h0.astype(f32), (states, chunk_decay))
    decay_out = jnp.exp(a_cum).transpose(0, 3, 4, 1, 2)
    y_off = jnp.einsum('bclgn,cbghpn->bclghp', cc, h_prev) * decay_out[..., None]
    y = (y_diag + y_off).reshape(bsz, L, H, P)
    return y, h_last

def ssd_mixer(h_lat, h_ctx, w_in, conv_w, conv_b, a_log, dt_bias, d_skip, gnorm_w, w_out, need_ctx_out):
    bsz = h_lat.shape[0]

    def project(h):
        L = h.shape[1]
        zxbcdt = h @ w_in
        z = zxbcdt[..., :D_INNER]
        xbc = zxbcdt[..., D_INNER:D_INNER + D_CONV_CH]
        dt = zxbcdt[..., D_INNER + D_CONV_CH:]
        xbc = jax.nn.silu(dwconv_centred(xbc, conv_w, conv_b))
        xs = xbc[..., :D_INNER].reshape(bsz, L, SSD_HEADS, SSD_HEAD_DIM)
        bm = xbc[..., D_INNER:D_INNER + SSD_GROUPS * D_STATE].reshape(bsz, L, SSD_GROUPS, D_STATE)
        cm = xbc[..., D_INNER + SSD_GROUPS * D_STATE:].reshape(bsz, L, SSD_GROUPS, D_STATE)
        dt = jax.nn.softplus(dt.astype(jnp.float32).reshape(bsz, L, 2, SSD_HEADS)
                             + dt_bias.astype(jnp.float32))
        return z, xs, bm, cm, dt

    def flip(t):
        return jnp.flip(t, axis=1)

    def finish(y, xs, z, ref):
        L = xs.shape[1]
        y = y + xs.astype(jnp.float32) * d_skip.astype(jnp.float32)[:, None]
        y = y.reshape(bsz, L, D_INNER)
        y = rmsnorm(y * jax.nn.silu(z.astype(jnp.float32)), gnorm_w)
        return (y @ w_out).astype(ref.dtype)

    a = -jnp.exp(a_log.astype(jnp.float32))
    h0 = jnp.zeros((bsz, SSD_GROUPS, SSD_HEADS_PER_GROUP, SSD_HEAD_DIM, D_STATE), jnp.float32)
    zc, xc, bcm, ccm, dtc = project(h_ctx)
    yc_f, sc_f = ssd_scan(xc, dtc[:, :, 0], a[0], bcm, ccm, h0)
    yc_b, sc_b = ssd_scan(flip(xc), flip(dtc[:, :, 1]), a[1], flip(bcm), flip(ccm), h0)
    zl, xl, bl, cl, dtl = project(h_lat)
    yl_f, _ = ssd_scan(xl, dtl[:, :, 0], a[0], bl, cl, sc_f)
    yl_b, _ = ssd_scan(flip(xl), flip(dtl[:, :, 1]), a[1], flip(bl), flip(cl), sc_b)
    out_lat = finish(yl_f + flip(yl_b), xl, zl, h_lat)
    out_ctx = finish(yc_f + flip(yc_b), xc, zc, h_ctx) if need_ctx_out else None
    return out_lat, out_ctx

def rope_2d(x, cos, sin):
    half = x.shape[-1] // 2
    c = cos[None, :, None, None, :].astype(x.dtype)
    s = sin[None, :, None, None, :].astype(x.dtype)
    x1, x2 = x[..., :half], x[..., half:]
    return jnp.concatenate([x1 * c - x2 * s, x2 * c + x1 * s], axis=-1)

def diff_attn(h_lat, h_ctx, w_qkv, w_o, lq1, lk1, lq2, lk2, subln_w, lambda_init, cos, sin, need_ctx_out):
    bsz = h_lat.shape[0]
    hq = DA_HEADS * 2 * DA_HEAD_DIM

    def project(h):
        L = h.shape[1]
        qkv = h @ w_qkv
        q = qkv[..., :hq].reshape(bsz, L, DA_HEADS, 2, DA_HEAD_DIM)
        k = qkv[..., hq:2 * hq].reshape(bsz, L, DA_HEADS, 2, DA_HEAD_DIM)
        v = qkv[..., 2 * hq:].reshape(bsz, L, DA_HEADS, DA_V_DIM)
        return q, k, v

    f32 = jnp.float32
    lam = (jnp.exp(jnp.sum(lq1.astype(f32) * lk1.astype(f32)))
           - jnp.exp(jnp.sum(lq2.astype(f32) * lk2.astype(f32))) + lambda_init)
    scale = DA_HEAD_DIM ** -0.5

    def attend(q, k, v):
        s = jnp.einsum('bqhmd,bkhmd->bhmqk', q, k, preferred_element_type=f32) * scale
        p = jax.nn.softmax(s, axis=-1)
        w = p[:, :, 0] - lam * p[:, :, 1]
        return jnp.einsum('bhqk,bkhe->bqhe', w.astype(v.dtype), v)

    def finish(o, ref):
        L = o.shape[1]
        o = rmsnorm(o, subln_w) * (1.0 - lambda_init)
        return (o.reshape(bsz, L, DA_HEADS * DA_V_DIM) @ w_o).astype(ref.dtype)

    qc, kc, vc = project(h_ctx)
    ql, kl, vl = project(h_lat)
    ql = rope_2d(ql, cos, sin)
    kl = rope_2d(kl, cos, sin)
    k_all = jnp.concatenate([kl, kc], axis=1)
    v_all = jnp.concatenate([vl, vc], axis=1)
    L = h_lat.shape[1]
    nb = L // Q_BLOCK
    q_blocks = ql.reshape(bsz, nb, Q_BLOCK, DA_HEADS, 2, DA_HEAD_DIM).transpose(1, 0, 2, 3, 4, 5)
    o_lat = lax.map(lambda qb: attend(qb, k_all, v_all), q_blocks)
    o_lat = o_lat.transpose(1, 0, 2, 3, 4).reshape(bsz, L, DA_HEADS, DA_V_DIM)
    out_lat = finish(o_lat, h_lat)
    out_ctx = finish(attend(qc, kc, vc), h_ctx) if need_ctx_out else None
    return out_lat, out_ctx

def axial_rope_tables(L):
    rows_n = L // GRID_W
    row = jnp.repeat(jnp.arange(rows_n, dtype=jnp.float32), GRID_W)
    col = jnp.tile(jnp.arange(GRID_W, dtype=jnp.float32), rows_n)
    freqs = 1.0 / (ROPE_THETA ** (jnp.arange(ROPE_PAIRS_PER_AXIS, dtype=jnp.float32) / ROPE_PAIRS_PER_AXIS))
    ang = jnp.concatenate([row[:, None] * freqs, col[:, None] * freqs], axis=-1)
    return jnp.cos(ang), jnp.sin(ang)

def setup_inputs(seed: int = 0) -> dict:
    key = jax.random.key(seed)
    ks = jax.random.split(key, 32)
    nrm = jax.random.normal
    f32 = jnp.float32
    D = D_MODEL
    dt0 = jnp.exp(jax.random.uniform(ks[10], (N_SSD_LAYERS, 2, SSD_HEADS), f32,
                                     math.log(1e-3), math.log(1e-1)))
    return {
        "x": nrm(ks[0], (BATCH, SEQ, D), f32),
        "c": nrm(ks[1], (BATCH, D), f32),
        "ctx": nrm(ks[2], (BATCH, CTX_LEN, D), f32),
        "c_ctx": nrm(ks[3], (D,), f32),
        "w_ada": nrm(ks[4], (DEPTH, D, 6 * D), f32) * (0.5 * D ** -0.5),
        "b_ada": nrm(ks[5], (DEPTH, 6 * D), f32) * 0.02,
        "norm1_w": 1.0 + 0.05 * nrm(ks[6], (DEPTH, D), f32),
        "norm2_w": 1.0 + 0.05 * nrm(ks[7], (DEPTH, D), f32),
        "ssd_w_in": nrm(ks[8], (N_SSD_LAYERS, D, D_IN_PROJ), f32) * D ** -0.5,
        "ssd_conv_w": nrm(ks[9], (N_SSD_LAYERS, CONV_W, D_CONV_CH), f32) * CONV_W ** -0.5,
        "ssd_conv_b": nrm(ks[11], (N_SSD_LAYERS, D_CONV_CH), f32) * 0.02,
        "ssd_a_log": jnp.log(jax.random.uniform(ks[12], (N_SSD_LAYERS, 2, SSD_HEADS), f32, 1.0, 16.0)),
        "ssd_dt_bias": dt0 + jnp.log(-jnp.expm1(-dt0)),
        "ssd_d": 1.0 + 0.05 * nrm(ks[13], (N_SSD_LAYERS, SSD_HEADS), f32),
        "ssd_norm_w": 1.0 + 0.05 * nrm(ks[14], (N_SSD_LAYERS, D_INNER), f32),
        "ssd_w_out": nrm(ks[15], (N_SSD_LAYERS, D_INNER, D), f32) * D_INNER ** -0.5,
        "da_w_qkv": nrm(ks[16], (N_ATTN_LAYERS, D, DA_QKV), f32) * D ** -0.5,
        "da_w_o": nrm(ks[17], (N_ATTN_LAYERS, DA_HEADS * DA_V_DIM, D), f32) * (DA_HEADS * DA_V_DIM) ** -0.5,
        "da_lq1": nrm(ks[18], (N_ATTN_LAYERS, DA_HEAD_DIM), f32) * 0.1,
        "da_lk1": nrm(ks[19], (N_ATTN_LAYERS, DA_HEAD_DIM), f32) * 0.1,
        "da_lq2": nrm(ks[20], (N_ATTN_LAYERS, DA_HEAD_DIM), f32) * 0.1,
        "da_lk2": nrm(ks[21], (N_ATTN_LAYERS, DA_HEAD_DIM), f32) * 0.1,
        "da_subln_w": 1.0 + 0.05 * nrm(ks[22], (N_ATTN_LAYERS, DA_V_DIM), f32),
        "ffn_w_gate": nrm(ks[23], (DEPTH, D, D_FF), f32) * D ** -0.5,
        "ffn_w_up": nrm(ks[24], (DEPTH, D, D_FF), f32) * D ** -0.5,
        "ffn_w_down": nrm(ks[25], (DEPTH, D_FF, D), f32) * D_FF ** -0.5,
        "final_norm_w": 1.0 + 0.05 * nrm(ks[26], (D,), f32),
    }

def reference(x, c, ctx, c_ctx, w_ada, b_ada, norm1_w, norm2_w, ssd_w_in, ssd_conv_w, ssd_conv_b,
              ssd_a_log, ssd_dt_bias, ssd_d, ssd_norm_w, ssd_w_out, da_w_qkv, da_w_o, da_lq1, da_lk1,
              da_lq2, da_lk2, da_subln_w, ffn_w_gate, ffn_w_up, ffn_w_down, final_norm_w):
    cos, sin = axial_rope_tables(x.shape[1])
    s_lat = jax.nn.silu(c)[:, None, :]
    s_ctx = jax.nn.silu(c_ctx)[None, None, :]
    x_lat, x_ctx = x, ctx
    for i in range(DEPTH):
        need_ctx = i < DEPTH - 1
        sh1, sc1, g1, sh2, sc2, g2 = jnp.split(s_lat @ w_ada[i] + b_ada[i], 6, axis=-1)
        csh1, csc1, cg1, csh2, csc2, cg2 = jnp.split(s_ctx @ w_ada[i] + b_ada[i], 6, axis=-1)
        a_lat = modulate(rmsnorm(x_lat, norm1_w[i]), sh1, sc1)
        a_ctx = modulate(rmsnorm(x_ctx, norm1_w[i]), csh1, csc1)
        j = i // N_MIXERS
        if i % N_MIXERS == 0:
            m_lat, m_ctx = ssd_mixer(a_lat, a_ctx, ssd_w_in[j], ssd_conv_w[j], ssd_conv_b[j],
                                     ssd_a_log[j], ssd_dt_bias[j], ssd_d[j], ssd_norm_w[j],
                                     ssd_w_out[j], need_ctx)
        else:
            lambda_init = 0.8 - 0.6 * math.exp(-0.3 * i)
            m_lat, m_ctx = diff_attn(a_lat, a_ctx, da_w_qkv[j], da_w_o[j], da_lq1[j], da_lk1[j],
                                     da_lq2[j], da_lk2[j], da_subln_w[j], lambda_init, cos, sin,
                                     need_ctx)
        x_lat = x_lat + g1 * m_lat
        f_lat = swiglu(modulate(rmsnorm(x_lat, norm2_w[i]), sh2, sc2),
                       ffn_w_gate[i], ffn_w_up[i], ffn_w_down[i])
        x_lat = x_lat + g2 * f_lat
        if need_ctx:
            x_ctx = x_ctx + cg1 * m_ctx
            f_ctx = swiglu(modulate(rmsnorm(x_ctx, norm2_w[i]), csh2, csc2),
                           ffn_w_gate[i], ffn_w_up[i], ffn_w_down[i])
            x_ctx = x_ctx + cg2 * f_ctx
    return rmsnorm(x_lat, final_norm_w)


_drawn_inputs = setup_inputs


def setup_inputs(seed=0):
    import zlib

    import numpy as np

    out = dict(_drawn_inputs(seed))
    spreads = {}
    factors = {'norm2_w': 2.74,
     'ssd_conv_b': 6.741,
     'ssd_d': 7.561,
     'ssd_norm_w': 3.742,
     'da_lq2': 7.921,
     'da_lk2': 5.549,
     'da_subln_w': 7.616}
    for name, (base, spread) in spreads.items():
        noise = np.random.default_rng([zlib.crc32(name.encode()), seed]).standard_normal(out[name].shape)
        drawn = base * np.exp(spread * noise) if base else spread * noise
        out[name] = __import__('jax').numpy.asarray(drawn.astype(out[name].dtype))
    for name, factor in factors.items():
        out[name] = (out[name] * factor).astype(out[name].dtype)
    return out
```

```python
import math
from contextlib import ExitStack

import numpy as np

import concourse.bass as bass
from concourse import mybir

F32 = mybir.dt.float32
F16 = mybir.dt.float16
BF16 = mybir.dt.bfloat16
ALU = mybir.AluOpType
ACT = mybir.ActivationFunctionType
AXX = mybir.AxisListType.X

P = 128
D = 1024
KC = D // P
TC = 256
T = 2 * TC
DI = 2048
NG = 4
NH = 32
HG = NH // NG
HP = 64
QT = DI // NG // P
NCH = T // P
FF = 2816
FC = FF // P
UN = 256
UF = KC * UN
EPS = 1e-6
WS = 64.0
AS = 16.0
FS = 4.0
DS = 16.0
LAMBDA_INIT = 0.8 - 0.6 * math.exp(-0.3)
NEG = -1e30
AHEADS = 8

_sizes = [("n1w", 2 * KC), ("n2w", 2 * KC), ("fnw", KC), ("bada", 96), ("conv", NG * 36), ("dskip", 16),
          ("gnw", 16), ("subln", 1), ("dtb", 64), ("alog", 64), ("lqk", 256), ("cvec", 2 * KC)]
COL, _at = {}, 0
for _n, _s in _sizes:
    COL[_n] = (_at, _at + _s)
    _at += _s
NCOL = _at
K_ID, K_ONE, K_PERM, K_COS, K_SIN, NKEEP = 0, 128, 256, 384, 640, 896
S_TF, S_TB, S_NF, S_NB, NSTAGE = 0, 128, 256, 384, 512

U_SSD0 = 0
U_GRP = 4
U_TAIL = U_GRP + 6 * (NG - 1)
U_OUT = U_TAIL + 2
U_GU0 = U_OUT + 8
U_DN0 = U_GU0 + FC
U_V = U_DN0 + 12
U_QK = U_V + 4
U_WO = U_QK + 8
U_GU1 = U_WO + 4
U_DN1 = U_GU1 + FC
DNK = [(0, 8), (8, 15), (15, 22)]
ADA_FIRST = 8
ADA_PE = ADA_FIRST + NG
ADA_OUT = 8
ADA_GU = FC


class Unit:

    def __init__(self, base, per=0, i=None):
        self.base, self.per, self.i = base, per, i
        self.slot = base % 2

    def plus(self, k):
        return Unit(self.base + k, self.per, self.i)

    @property
    def n(self):
        return self.base if self.i is None else self.i * self.per + self.base

    @property
    def half(self):
        return self.base * 2 if self.i is None else self.i * (self.per * 2) + self.base * 2

    @property
    def turn(self):
        return self.base // 2 if self.i is None else self.i * (self.per // 2) + self.base // 2


def build(nc, cols, keep, stage, xT, wada, wadaT, crow, wdt, wxg, wz, wout, wgu, wdn, wv, wqk, wo, out):
    ctx = ExitStack()
    with ctx:
        def sb(name, shape, dt=F32):
            return ctx.enter_context(nc.sbuf_tensor(name, shape, dt))

        def sem(name):
            return ctx.enter_context(nc.semaphore(name))

        x = sb("x", [P, KC, T])
        hh = sb("hh", [P, KC, T], F16)
        hl = sb("hl", [P, KC, T], F16)
        raw = sb("raw", [P, 2, UF])
        wh = sb("wh", [P, 2, UF], F16)
        wl = sb("wl", [P, 2, UF], F16)
        araw = sb("araw", [P, UF])
        col = sb("col", [P, NCOL])
        kp = sb("kp", [P, NKEEP])
        masks = sb("masks", [P, 3, P], F16)
        negm = sb("negm", [P, 2, P], BF16)
        idb = sb("idb", [P, P], BF16)
        s2 = sb("s2", [P, KC, 2])
        adac = sb("adac", [P, 2, 48, 2])
        wsc = sb("wsc", [P, KC, 2])
        wsh = sb("wsh", [P, KC, 2])
        gcol = sb("gcol", [P, KC, 2])
        small = sb("small", [P, 64])
        sq = sb("sq", [P, 2, T])
        ssq = sb("ssq", [P, T])
        AR = 30640
        arena = sb("arena", [P, AR])
        at = [0]

        def carve(n):
            a = at[0]
            at[0] += n
            assert at[0] <= AR, at[0]
            return arena[:, a:a + n]

        nt = carve(2 * T).rearrange("p (b t) -> p b t", b=2)
        n32 = carve(2 * T).rearrange("p (b t) -> p b t", b=2)
        rdg = carve(T)
        mark = at[0]
        afirst = arena[:, mark:mark + ADA_FIRST * UF].rearrange("p (u f) -> p u f", u=ADA_FIRST)
        stg = arena[:, mark + ADA_FIRST * UF:mark + ADA_FIRST * UF + NSTAGE]
        ya, yb = nt[:, 0, :], nt[:, 1, :]
        gt = n32
        G = carve(16 * T).rearrange("p (q t) -> p q t", q=16)
        pre = carve(2 * 520).rearrange("p (b s t) -> p b s t", b=2, s=2)
        acc = rdg
        xbc = carve(6 * T).rearrange("p (q t) -> p q t", q=6)
        xD = carve(QT * T).rearrange("p (q t) -> p q t", q=QT)
        Cc, Bt, cb = carve(T), carve(T), carve(T).rearrange("p (c l) -> p c l", c=NCH)
        xd = carve(2 * NCH * 512).rearrange("p (c d f) -> p c d f", c=NCH, d=2)
        xdd = carve(2 * 512).rearrange("p (b f) -> p b f", b=2)
        Hs = carve(6 * 512).rearrange("p (k f) -> p k f", k=6)
        E = carve(2 * 512).rearrange("p (b h l) -> p b h l", b=2, h=4)
        ys = carve(2 * 512).rearrange("p (b f) -> p b f", b=2)
        PR = carve(5 * 256).rearrange("p (q c h) -> p q c h", q=5, c=8)
        PRg = carve(5 * 64).rearrange("p (q c h) -> p q c h", q=5, c=8)
        dg = carve(4)
        adh = carve(128).bitcast(F16)
        adl = carve(128).bitcast(F16)
        adgh = carve(32).bitcast(F16)
        adgl = carve(32).bitcast(F16)
        DT, DST, DOUT, NEGA, DCH = range(5)
        dtraw = E[:, 0, :, :].rearrange("p h l -> p (h l)")
        dth = E[:, 1, 0:2, :].rearrange("p h l -> p (h l)").bitcast(F16)
        dtl = E[:, 1, 2:4, :].rearrange("p h l -> p (h l)").bitcast(F16)
        dx, de = ys[:, 0, 0:256], ys[:, 0, 256:512]
        dz, dz2 = ys[:, 1, 0:256], ys[:, 1, 256:512]
        dq, dr = xdd[:, 0, 0:256], xdd[:, 0, 256:512]
        da = xdd[:, 1, 0:64]
        gb = mark + 16 * T
        gh = arena[:, gb:gb + 4096].bitcast(F16).rearrange("p (q t) -> p q t", q=16)
        gl = arena[:, gb + 4096:gb + 8192].bitcast(F16).rearrange("p (q t) -> p q t", q=16)
        at[0] = gb + 8192
        abuf = carve(2 * UF).rearrange("p (b m k) -> p b m k", b=2, m=2)
        adump = carve(4 * D // 2).bitcast(BF16).rearrange("p (a k) -> p a k", a=4)
        at[0] = mark
        ah = carve(FC * T // 2).bitcast(F16).rearrange("p (q t) -> p q t", q=FC)
        al = carve(FC * T // 2).bitcast(F16).rearrange("p (q t) -> p q t", q=FC)
        sg = carve(2 * T).rearrange("p (b t) -> p b t", b=2)
        a32 = carve(2 * T).rearrange("p (b t) -> p b t", b=2)
        at[0] = mark
        v = carve(4 * D).rearrange("p (c f) -> p c f", c=4)
        qst, qr = carve(512).rearrange("p (h t) -> p h t", h=2), carve(512).rearrange("p (h t) -> p h t", h=2)
        kst, kr = carve(1024).rearrange("p (h t) -> p h t", h=2), carve(1024).rearrange("p (h t) -> p h t", h=2)
        r1, r2 = carve(512).rearrange("p (h t) -> p h t", h=2), carve(512).rearrange("p (h t) -> p h t", h=2)
        EA = carve(4 * 512).rearrange("p (b m k) -> p b m k", b=2, m=2)
        wmt = carve(2 * 512).rearrange("p (b k) -> p b k", b=2)
        wT = carve(2 * 512).rearrange("p (b k) -> p b k", b=2)
        osb = carve(2 * D).rearrange("p (b h e) -> p b h e", b=2, h=AHEADS)
        osq = carve(128)
        o32 = carve(2 * 512).rearrange("p (b f) -> p b f", b=2)
        oh = carve(1024).bitcast(F16).rearrange("p (h t) -> p h t", h=AHEADS)
        ol = carve(1024).bitcast(F16).rearrange("p (h t) -> p h t", h=AHEADS)
        mx = carve(4).rearrange("p (b m) -> p b m", b=2)
        nb = carve(4).rearrange("p (b m) -> p b m", b=2)
        es = carve(4).rearrange("p (b m) -> p b m", b=2)
        rs = carve(4).rearrange("p (b m) -> p b m", b=2)
        oss = carve(16).rearrange("p (b h) -> p b h", b=2)
        ort = carve(16).rearrange("p (b h) -> p b h", b=2)
        lp = carve(128).rearrange("p (a d) -> p a d", a=2)
        ls = carve(2)
        nlam = carve(1)
        fin = arena[:, mark:mark + KC * TC].rearrange("p (k t) -> p k t", k=KC)

        ident, ones, perm = kp[:, K_ID:K_ID + P], kp[:, K_ONE:K_ONE + P], kp[:, K_PERM:K_PERM + P]
        cosT, sinT = kp[:, K_COS:K_COS + TC], kp[:, K_SIN:K_SIN + TC]
        eps = small[:, 0:1]
        rt = small[:, 4:8]

        def cc(name, a=0, b=None):
            lo, hi = COL[name]
            return col[:, lo + a:(hi if b is None else lo + b)]

        bank = [ctx.enter_context(nc.psum_tensor(f"bank{i}", [P, 512], F32)) for i in range(8)]
        GB = bank[0:4]
        DB = bank[2:4]
        YB, OB, AB = bank[4], bank[5:7], bank[7]
        SB = [(bank[2], bank[3]), (bank[5], bank[6])]
        OTB = [bank[2], bank[3], bank[5], bank[6]]

        in_col, in_kp, in_stage, in_x, in_dt = [sem(n) for n in ("in_col", "in_kp", "in_stage", "in_x", "in_dt")]
        in_ada = [sem(f"in_ada{i}") for i in range(4)]
        raw_in = [sem("raw_in0"), sem("raw_in1")]
        araw_in, out_done = sem("araw_in"), sem("out_done")
        crow_in, srow_ok = sem("crow_in"), sem("srow_ok")
        abuf_in = [sem("abuf_in0"), sem("abuf_in1")]
        ada_sum, ada_ok = sem("ada_sum"), sem("ada_ok")
        hi_done, lo_done = sem("hi_done"), sem("lo_done")
        unit_done = sem("unit_done")
        LO = UD = 4
        masks_ok, s2_ok, eps_ok = sem("masks_ok"), sem("s2_ok"), sem("eps_ok")
        a0_mm = sem("a0_mm")
        cols_ok = sem("cols_ok")
        sqd, ssd = sem("sqd"), sem("ssd")
        c_ss, c_rt, c_rr, c_dg, c_bc = [sem(n) for n in ("c_ss", "c_rt", "c_rr", "c_dg", "c_bc")]
        nt_ok, n32_ok, hh_ok, h_ok = sem("nt_ok"), sem("n32_ok"), sem("hh_ok"), sem("h_ok")
        xup = sem("xup")
        dth_ok, dtl_ok, dt_mm, dta, dtv, adt_ok = [sem(n) for n in ("dth_ok", "dtl_ok", "dt_mm", "dta", "dtv", "adt_ok")]
        A_mm, aexp, pr_ok, pads_ok = sem("A_mm"), sem("aexp"), sem("pr_ok"), sem("pads_ok")
        pre_ok, conv, conv_ok, xbc_ok, zs_ok = [sem(n) for n in ("pre_ok", "conv", "conv_ok", "xbc_ok", "zs_ok")]
        o_mm = [sem("o_mm0"), sem("o_mm1")]
        o_free = [sem("o_free0"), sem("o_free1")]
        prg_ok, xD_ok, xdd_ok, hm_ok, bt_ok = [sem(n) for n in ("prg_ok", "xD_ok", "xdd_ok", "hm_ok", "bt_ok")]
        d_mm, e_ok, t_ok, yd = sem("d_mm"), sem("e_ok"), sem("t_ok"), sem("yd")
        yp, y_ok = sem("yp"), sem("y_ok")
        a_mm, a_free = sem("a_mm"), sem("a_free")
        g_ok = sem("g_ok")
        gn_t, gn_h, gn_ok = sem("gn_t"), sem("gn_h"), sem("gn_ok")
        sg_ok, a32_ok, ah_ok, al_ok = sem("sg_ok"), sem("a32_ok"), sem("ah_ok"), sem("al_ok")
        v_ok, qk_ok, rot_mm, rope, qkr_ok, lam = [sem(n) for n in ("v_ok", "qk_ok", "rot_mm", "rope", "qkr_ok", "lam")]
        s_mm, mx_ok, nb_ok, ea_ok, rs_ok, w_t, w_ok = [sem(n) for n in ("s_mm", "mx_ok", "nb_ok", "ea_ok", "rs_ok", "w_t", "w_ok")]
        wt_mm, wt_ok, pv_mm, os_ok = sem("wt_mm"), sem("wt_ok"), sem("pv_mm"), sem("os_ok")
        ort_s, ort_ok, on_ok, ot_mm, o32_ok, oh_ok, o_ok = [sem(n) for n in ("ort_s", "ort_ok", "on_ok", "ot_mm", "o32_ok", "oh_ok", "o_ok")]
        fin_ok = sem("fin_ok")
        apart = sem("apart")

        O_PER = 9
        O_XT = [(0, 0), (1, 0), (0, 1), (1, 1)]
        O_B, O_CB = (0, 2), (1, 2)
        O_ST = [(0, 3), (1, 3), (0, 4), (1, 4), (0, 5), (1, 5)]
        ST = [(0, 0), (1, 1), (1, 0), (0, 1), (2, 0), (3, 1)]
        ST_FROM = [None, None, 0, 1, 2, 3]
        YOFF = [{1: (1, 6)}, {0: (0, 6)}, {0: (2, 7), 1: (5, 7)}, {0: (4, 8), 1: (3, 8)}]
        A_PER = 5
        A_ADA = 0
        A_YT = [1, 2, 3, 4]
        SQ_G = KC
        SQ_X = [0, None, SQ_G + 16, SQ_G + 16 + KC, SQ_G + 16 + 2 * KC, SQ_G + 16 + 3 * KC]
        HN = {0: 0, 2: 1, 3: 2, 4: 3}

        block = ctx.enter_context(nc.Block())

        @block.sync
        def _(sp):
            sp.dma_start(col[:, :], cols).then_inc(in_col, 16)
            for b in range(4):
                sp.dma_start(afirst[:, 2 * b:2 * b + 2, :], wada[2 * b:2 * b + 2].rearrange("u p f -> p u f")).then_inc(in_ada[b], 16)
                if b == 0:
                    sp.dma_start(x[:, :, :], xT).then_inc(in_x, 16)
                    sp.dma_start(kp[:, :], keep).then_inc(in_kp, 16)
                    sp.dma_start(stg, stage).then_inc(in_stage, 16)
            sp.dma_start(dtraw, wdt).then_inc(in_dt, 16)

            def load(u, src, n=UF):
                sp.wait_ge(lo_done, u.half + 2)
                sp.dma_start(raw[:, u.slot, 0:n], src).then_inc(raw_in[u.slot], 16)

            def load_group(u, g):
                for k, (a, b) in enumerate([(0, 1024), (1024, 2048), (2048, 4096), (4096, 6144)]):
                    load(u.plus(k), wxg[g, :, a:b], b - a)

            load_group(Unit(U_SSD0), 0)
            with sp.Fori(0, NG - 1) as g:
                u = Unit(U_GRP, 6, g)
                load(u, wz[g * 2])
                load(u.plus(1), wz[g * 2 + 1])
                load_group(u.plus(2), g + 1)
            for k in range(2):
                load(Unit(U_TAIL + k), wz[2 * (NG - 1) + k])

            def pairs(n, first, src, at=0):
                with sp.Fori(0, n) as i:
                    for k in range(2):
                        load(Unit(first + k, 2, i), src[i * 2 + (at + k)])

            def ffn(layer, ugu, udn):
                pairs(FC // 2, ugu, wgu, layer * FC)
                for m in range(4):
                    for k, (a, b) in enumerate(DNK):
                        load(Unit(udn + 3 * m + k), wdn[layer * 4 + m, :, a * UN:b * UN], (b - a) * UN)

            pairs(4, U_OUT, wout)
            ffn(0, U_GU0, U_DN0)
            pairs(2, U_V, wv)
            pairs(4, U_QK, wqk)
            pairs(2, U_WO, wo)
            ffn(1, U_GU1, U_DN1)
            for b in range(2):
                sp.wait_ge(fin_ok, 4 * b + 4)
                sp.dma_start(out[:, 4 * b:4 * b + 4, :], fin[:, 4 * b:4 * b + 4, :]).then_inc(out_done, 16)
            sp.wait_ge(out_done, 32)

        @block.scalar
        def _(act):
            def alone():
                act.sem_inc(apart, 1)

            def cvt_half(u, j, a, b):
                if j == 0:
                    act.wait_ge(raw_in[u.slot], u.turn * 16 + 16)
                act.wait_ge(unit_done, u.half + (UD - 3 + j))
                act.activation(wh[:, u.slot, a:b], raw[:, u.slot, a:b], ACT.Copy, scale=WS).then_inc(hi_done, 1)

            def cvt(u, n=UF):
                cvt_half(u, 0, 0, n // 2)
                cvt_half(u, 1, n // 2, n)

            def cvt_on(u, n=UF):
                cvt_half(u, 1, UF // 2, n)
                if u.base < U_DN1 + 11:
                    cvt_half(u.plus(1), 0, 0, UF // 2)

            def ada_load(a, last):
                act.wait_ge(a_mm, last + 3)
                act.dma_start(araw[:, :], wada[a]).then_inc(araw_in, 16)

            def root(n, width, cs):
                act.wait_ge(c_ss, n + 1)
                act.activation(rt[:, cs:4], OB[0][:, cs:4], ACT.Sqrt, scale=1.0 / width, bias=eps).then_inc(c_rt, 1)

            def square_pair(n, k, t0, up):
                for m in range(2):
                    act.wait_ge(xup, up + (m + 5))
                    act.wait_ge(ssd, n + (m - 1))
                    alone()
                    act.activation(sq[:, m, None, t0:T], x[:, bass.ds(k + m, 1), t0:T], ACT.Square).then_inc(sqd, 1)

            def h_hi(n, t0):
                for k in range(KC):
                    act.wait_ge(n32_ok, HN[n] * KC + k + 1)
                    act.activation(hh[:, k, t0:T], n32[:, k % 2, t0:T], ACT.Copy).then_inc(hh_ok, 1)

            def evac_pre(u, g, tile, b):
                act.wait_ge(unit_done, u.half + (UD + 2))
                act.wait_ge(conv_ok, g * 6 + (tile + 1))
                act.activation(pre[:, tile % 2, :, 2:258], GB[b][:, :].rearrange("p (s t) -> p s t", s=2), ACT.Copy,
                               scale=1.0 / (WS * AS)).then_inc(pre_ok, 1)

            def silu_xbc(g, tile):
                act.wait_ge(conv_ok, g * 6 + (tile + 3))
                if tile == 0 and not isinstance(g, int):
                    act.wait_ge(xD_ok, g * QT)
                act.activation(xbc[:, tile, :], acc, ACT.Silu).then_inc(xbc_ok, 1)

            def exps(g, c, between=None):
                for q in range(4):
                    n = g * 16 + (4 * c + q)
                    d, hq = q % 2, q // 2
                    act.wait_ge(d_mm, n + 1)
                    act.wait_ge(yd, n + 1)
                    for h in range(4):
                        i = act.activation(E[:, q % 2, h, :], DB[q % 2][:, h * P:(h + 1) * P], ACT.Exp, scale=1.0 / DS,
                                           bias=PRg[:, NEGA, 2 * c + d, 4 * hq + h:4 * hq + h + 1])
                    i.then_inc(e_ok, 1)
                    if between and q in between:
                        between[q]()

            def z_out(u, g, k):
                act.wait_ge(unit_done, u.half + (UD + 2))
                alone()
                for m in range(2):
                    act.activation(G[:, bass.ds(g * QT + (2 * k + m), 1), :], GB[m][:, None, :], ACT.Silu,
                                   scale=1.0 / (WS * AS)).then_inc(zs_ok, 1)

            def group(g, u, more):
                cvt(u.plus(1))
                act.wait_ge(o_mm[0], g * O_PER + (O_B[1] + 1))
                act.activation(Bt, OB[0][:, :], ACT.Copy).then_inc(o_free[0], 1)
                act.wait_ge(o_mm[1], g * O_PER + (O_CB[1] + 1))
                act.activation(cb.rearrange("p c l -> p (c l)"), OB[1][:, :], ACT.Copy).then_inc(o_free[1], 1)
                act.activation(Cc, xbc[:, 1, :], ACT.Copy).then_inc(bt_ok, 1)
                z_out(u, g, 0)
                ada_load(g + ADA_FIRST, g * A_PER - 1)
                cvt(u.plus(2), 1024 if more else UF)
                for k in range(2):
                    act.wait_ge(o_mm[k], g * O_PER + (O_ST[k][1] + 1))
                    act.activation(Hs[:, k, :], OB[k][:, :], ACT.Copy).then_inc(o_free[k], 1)
                z_out(u.plus(1), g, 1)
                if more:
                    cvt(u.plus(3), 1024)
                exps(g, 0)
                if more:
                    evac_pre(u.plus(2), g + 1, 0, 0)
                    cvt(u.plus(4))
                exps(g, 1, {1: lambda: silu_xbc(g + 1, 0)} if more else None)
                if more:
                    evac_pre(u.plus(3), g + 1, 1, 1)
                    cvt(u.plus(5))
                exps(g, 2, {1: lambda: silu_xbc(g + 1, 1)} if more else None)
                if more:
                    for m in range(2):
                        evac_pre(u.plus(4), g + 1, 2 + m, m)
                    cvt(u.plus(6))
                if not more:
                    act.wait_ge(a_mm, g * A_PER + (A_ADA + 3))
                    act.dma_start(araw[:, :], crow).then_inc(crow_in, 16)
                exps(g, 3, {1: lambda: silu_xbc(g + 1, 2), 3: lambda: silu_xbc(g + 1, 3)} if more else None)
                if more:
                    for m in range(2):
                        evac_pre(u.plus(5), g + 1, 4 + m, m)
                act.wait_ge(g_ok, g * NCH + (NCH + 2))
                for q in range(QT):
                    act.wait_ge(ssd, g * QT + (SQ_G + q - 1))
                    alone()
                    act.activation(sq[:, q % 2, None, :], G[:, bass.ds(g * QT + q, 1), :], ACT.Square).then_inc(sqd, 1)
                if more:
                    silu_xbc(g + 1, 4)
                    silu_xbc(g + 1, 5)

            for s, n in [(e_ok, 2), (sg_ok, 2), (v_ok, 4), (qk_ok, 1), (ea_ok, 2), (wt_ok, 1), (os_ok, 1)]:
                act.sem_inc(s, n)
            act.wait_ge(in_col, 16)
            act.activation(s2[:, :, :], cc("cvec").rearrange("p (k b) -> p k b", b=2), ACT.Silu).then_inc(s2_ok, 1)
            act.wait_ge(in_stage, 16)
            act.activation(masks[:, 0:2, :], stg[:, S_TF:S_TF + 256].rearrange("p (a l) -> p a l", a=2), ACT.Copy).then_inc(masks_ok, 1)
            act.activation(negm[:, :, :], stg[:, S_NF:S_NF + 256].rearrange("p (a l) -> p a l", a=2), ACT.Copy).then_inc(masks_ok, 1)
            act.wait_ge(in_kp, 16)
            act.activation(masks[:, 2, :], ones, ACT.Copy).then_inc(masks_ok, 1)
            act.activation(idb[:, :], ident, ACT.Copy).then_inc(masks_ok, 1)
            act.wait_ge(in_x, 16)
            for k in range(KC):
                if k >= 2:
                    act.wait_ge(ssd, k - 1)
                act.activation(sq[:, k % 2, :], x[:, k, :], ACT.Square).then_inc(sqd, 1)
            act.wait_ge(eps_ok, 1)
            root(0, D, 0)
            act.wait_ge(in_dt, 16)
            act.activation(dth, dtraw, ACT.Copy, scale=WS).then_inc(dth_ok, 1)
            cvt(Unit(U_SSD0), 1024)
            h_hi(0, 0)
            cvt(Unit(U_SSD0 + 1), 1024)

            act.wait_ge(dtv, 1)
            act.activation(de, dx, ACT.Abs).then_inc(dta, 1)
            act.wait_ge(dta, 1)
            act.activation(de, de, ACT.Exp, scale=-1.0).then_inc(dta, 1)
            act.activation(da, cc("alog"), ACT.Exp).then_inc(dta, 1)

            u = Unit(U_SSD0)
            act.wait_ge(pads_ok, 2)
            evac_pre(u, 0, 0, 0)
            cvt(u.plus(2))
            silu_xbc(0, 0)
            evac_pre(u.plus(1), 0, 1, 1)
            cvt(u.plus(3))
            silu_xbc(0, 1)
            for m in range(2):
                evac_pre(u.plus(2), 0, 2 + m, m)
                silu_xbc(0, 2 + m)
            act.wait_ge(A_mm, 1)
            act.activation(PR[:, DOUT].rearrange("p c h -> p (c h)"), OB[1][:, 0:256], ACT.Exp, scale=1.0 / DS).then_inc(aexp, 1)
            act.activation(PR[:, DCH].rearrange("p c h -> p (c h)"), OB[1][:, 256:512], ACT.Exp, scale=1.0 / DS).then_inc(aexp, 1)
            act.wait_ge(pr_ok, 2)
            dst = PR[:, DST].rearrange("p c h -> p (c h)")
            act.activation(dst, dst, ACT.Exp).then_inc(aexp, 1)
            cvt(u.plus(4))
            for m in range(2):
                evac_pre(u.plus(3), 0, 4 + m, m)
                silu_xbc(0, 4 + m)
            with act.Fori(0, NG - 1) as g:
                group(g, Unit(U_GRP, 6, g), True)
            group(NG - 1, Unit(U_TAIL), False)

            cvt_half(Unit(U_OUT + 1), 0, 0, UF // 2)
            act.wait_ge(crow_in, 16)
            act.activation(araw[:, :], araw[:, :], ACT.Silu).then_inc(srow_ok, 1)
            root(1, DI, 0)
            for k in range(16):
                act.wait_ge(gn_t, k + 1)
                act.activation(gh[:, k, :], nt[:, k % 2, :], ACT.Copy).then_inc(gn_h, 1)
            with act.Fori(0, 2) as i:
                for m in range(2):
                    u = Unit(U_OUT + 2 * m, 4, i)
                    cvt_on(u.plus(1))
                    cvt_on(u.plus(2))
                    square_pair(i * 4 + (SQ_X[2] + 2 * m), i * 4 + 2 * m, 0, i * 4 + 2 * m)

            def ffn(layer, ugu, udn, t0, with_ada):
                n0 = layer * FC
                with act.Fori(0, FC // 2) as i:
                    u = Unit(ugu, 2, i)
                    cvt_on(u.plus(1))
                    act.wait_ge(unit_done, u.half + (UD + 2))
                    for m in range(2):
                        act.wait_ge(a32_ok, i * 2 + (n0 + m + 1))
                        act.activation(sg[:, m, t0:T], GB[m][:, t0:T], ACT.Silu, scale=1.0 / (WS * AS)).then_inc(sg_ok, 1)
                    cvt_on(u.plus(2))
                    for m in range(2):
                        act.wait_ge(a32_ok, i * 2 + (n0 + m + 3))
                        alone()
                        act.activation(ah[:, bass.ds(i * 2 + m, 1), t0:T], a32[:, m, None, t0:T], ACT.Copy).then_inc(ah_ok, 1)
                for m in range(4):
                    for k in range(3):
                        nxt = Unit(udn + 3 * m + k + 1)
                        if nxt.base < U_DN1 + 12:
                            kk = (3 * m + k + 1) % 12 % 3
                            a, b = DNK[kk]
                            cvt_on(nxt, UF if 3 * m + k + 1 == 12 else (b - a) * UN)
                    square_pair(SQ_X[3 + 2 * layer] + 2 * m, 2 * m, t0, 8 + 16 * layer + 2 * m)

            root(2, D, 0)
            h_hi(2, 0)
            ffn(0, U_GU0, U_DN0, 0, True)

            root(3, D, 0)
            h_hi(3, 0)
            act.wait_ge(lam, 2)
            act.activation(ls, ls, ACT.Exp).then_inc(lam, 1)
            with act.Fori(0, 2) as i:
                cvt_on(Unit(U_V + 1, 2, i))
                cvt_on(Unit(U_V + 2, 2, i))
                act.wait_ge(unit_done, i * 4 + (2 * U_V + UD + 4))
                alone()
                for c in range(4):
                    act.activation(v[:, c, bass.ds(i * 512, 512)], GB[c][:, :], ACT.Copy, scale=1.0 / (WS * AS)).then_inc(v_ok, 1)

            def q_out(u, i):
                act.wait_ge(unit_done, u.half + (UD + 2))
                act.wait_ge(qkr_ok, i + 1)
                for m in range(2):
                    act.activation(qst[:, m, :], GB[m][:, 0:TC], ACT.Copy, scale=1.0 / (WS * AS)).then_inc(qk_ok, 1)

            def k_out(u, i):
                act.wait_ge(unit_done, u.half + (UD + 2))
                for m in range(2):
                    act.activation(kst[:, m, :], GB[m][:, :], ACT.Copy, scale=1.0 / (WS * AS)).then_inc(qk_ok, 1)

            def exp_maps(i, n):
                N = i * 4 + n
                act.wait_ge(nb_ok, N + 1)
                act.wait_ge(w_ok, N + 1)
                for m in range(2):
                    s = act.activation(EA[:, n % 2, m, :], SB[n % 2][m][:, :], ACT.Exp, scale=0.125, bias=nb[:, n % 2, m:m + 1],
                                       accum_out=es[:, n % 2, m:m + 1])
                s.then_inc(ea_ok, 1)

            def wt_out(i, n):
                act.wait_ge(wt_mm, i * 4 + (n + 3))
                act.activation(wT[:, n % 2, :], YB[:, :], ACT.Copy).then_inc(wt_ok, 1)

            def o_out(i, n):
                head, qb = i * 2 + n // 2, n % 2
                act.wait_ge(pv_mm, i * 4 + (n + 1))
                act.wait_ge(os_ok, i * 4 + (n + 1))
                alone()
                act.activation(osb[:, qb, bass.ds(head, 1), :], AB[:, None, 0:P], ACT.Copy)
                act.activation(osq, AB[:, 0:P], ACT.Square, accum_out=oss[:, qb, bass.ds(head, 1)]).then_inc(os_ok, 1)

            cvt_on(Unit(U_QK + 1))
            q_out(Unit(U_QK), 0)
            cvt_on(Unit(U_QK + 2))
            k_out(Unit(U_QK + 1), 0)
            with act.Fori(1, 4) as i:
                u = Unit(U_QK, 2, i)
                j = i - 1
                cvt_on(u.plus(1))
                exp_maps(j, 0)
                exp_maps(j, 1)
                wt_out(j, 0)
                o_out(j, 0)
                exp_maps(j, 2)
                q_out(u, i)
                wt_out(j, 1)
                o_out(j, 1)
                cvt_on(u.plus(2))
                exp_maps(j, 3)
                wt_out(j, 2)
                o_out(j, 2)
                wt_out(j, 3)
                o_out(j, 3)
                k_out(u.plus(1), i)
            exp_maps(3, 0)
            for n in range(4):
                if n < 3:
                    exp_maps(3, n + 1)
                wt_out(3, n)
                o_out(3, n)
            act.wait_ge(os_ok, 17)
            act.activation(ort.rearrange("p b h -> p (b h)"), oss.rearrange("p b h -> p (b h)"), ACT.Sqrt, scale=1.0 / P, bias=eps).then_inc(ort_s, 1)
            for j in range(4):
                hq, qb = j // 2, j % 2
                act.wait_ge(o32_ok, j + 1)
                act.activation(oh[:, 4 * hq:4 * hq + 4, qb * P:(qb + 1) * P], o32[:, j % 2, :].rearrange("p (h t) -> p h t", h=4), ACT.Copy).then_inc(oh_ok, 1)
            with act.Fori(0, 2) as i:
                for m in range(2):
                    cvt_on(Unit(U_WO + m + 1, 2, i))
                    square_pair(i * 4 + (SQ_X[4] + 2 * m), i * 4 + 2 * m, TC, i * 4 + (16 + 2 * m))
            root(4, D, 2)
            h_hi(4, TC)
            ffn(1, U_GU1, U_DN1, TC, False)
            root(5, D, 2)

        @block.vector
        def _(ve):
            steps = [0]

            def step(i):
                i.then_inc(cols_ok, 1)
                steps[0] += 1
                ve.wait_ge(cols_ok, steps[0])

            def cvt_half(u, j, a, b):
                ve.wait_ge(hi_done, u.half + (j + 1))
                ve.scalar_tensor_tensor(wl[:, u.slot, a:b], raw[:, u.slot, a:b], WS, wh[:, u.slot, a:b], ALU.mult,
                                        ALU.subtract).then_inc(lo_done, 1)

            def cvt(u, n=UF):
                cvt_half(u, 0, 0, n // 2)
                cvt_half(u, 1, n // 2, n)

            def cvt_on(u, n=UF):
                cvt_half(u, 1, UF // 2, n)
                if u.base < U_DN1 + 11:
                    cvt_half(u.plus(1), 0, 0, UF // 2)

            asum = small[:, 40:44].rearrange("p (m c) -> p m c", m=2)
            adaf = adac[:, :, :, :].rearrange("p l c b -> p (l c) b")

            def ada_out(a, fill):
                ve.wait_ge(a_mm, fill + 3)
                bias = cc("bada")[:, bass.ds(a * 2, 2)]
                ve.tensor_tensor(adaf[:, bass.ds(a * 2, 2), :], AB[:, 0:4].rearrange("p (c b) -> p c b", b=2),
                                 bias[:, :, None].to_broadcast([P, 2, 2]), ALU.add).then_inc(a_free, 1)

            def ada_unit(k, b):
                ve.wait_ge(abuf_in[b], k * 8 + (16 - 8 * b))
                ve.wait_ge(ada_ok, k)
                for m in range(2):
                    for c in range(2):
                        i = ve.scalar_tensor_tensor(adump[:, 2 * m + c, :], abuf[:, b, m, :], 1.0, araw[:, c * D:(c + 1) * D], ALU.mult, ALU.mult,
                                                    accum_out=asum[:, m, c:c + 1])
                i.then_inc(ada_sum, 1)
                ve.wait_ge(ada_sum, k + 1)
                at_ = bass.ds(k * 2 + 2 * ADA_PE, 2)
                ve.tensor_tensor(adaf[:, at_, :], asum, cc("bada")[:, at_][:, :, None].to_broadcast([P, 2, 2]), ALU.add).then_inc(ada_ok, 1)

            def columns(l, norm_w, shift):
                step(ve.scalar_tensor_tensor(wsc[:, :, :], adac[:, l, shift + KC:shift + 2 * KC, :], 1.0,
                                             norm_w[:, :, None].to_broadcast([P, KC, 2]), ALU.add, ALU.mult))
                step(ve.tensor_scalar(wsc[:, :, :], wsc[:, :, :], AS, None, ALU.mult))
                step(ve.tensor_scalar(wsh[:, :, :], adac[:, l, shift:shift + KC, :], AS, None, ALU.mult))

            def gates(l, at, scale):
                step(ve.tensor_scalar(gcol[:, :, :], adac[:, l, at:at + KC, :], 1.0 / scale, None, ALU.mult))

            def inverse(n, cs):
                ve.wait_ge(c_rt, n + 1)
                ve.reciprocal(rt[:, cs:4], rt[:, cs:4]).then_inc(c_rr, 1)
                ve.wait_ge(c_rr, n + 1)
                ve.tensor_tensor(rdg[:, cs * P:T].rearrange("p (c l) -> p c l", l=P),
                                 ident[:, None, :].to_broadcast([P, 4 - cs, P]),
                                 rt[:, cs:4][:, :, None].to_broadcast([P, 4 - cs, P]), ALU.mult).then_inc(c_dg, 1)

            def add_square(n, t0, b):
                ve.wait_ge(sqd, n + 1)
                ve.wait_ge(ssd, n)
                ve.tensor_tensor(ssq[:, t0:T], ssq[:, t0:T], sq[:, b, t0:T], ALU.add).then_inc(ssd, 1)

            def h_lo(n, t0):
                m = HN[n] * KC
                kinds = [(0, 0, TC), (1, TC, T)][t0 // TC:]

                def lo(k):
                    ve.wait_ge(hh_ok, m + k + 1)
                    ve.tensor_tensor(hl[:, k, t0:T], n32[:, k % 2, t0:T], hh[:, k, t0:T], ALU.subtract).then_inc(h_ok, 1)

                ve.wait_ge(c_bc, n + 1)
                for k in range(KC):
                    ve.tensor_tensor(nt[:, k % 2, t0:T], x[:, k, t0:T], OB[1][:, t0:T], ALU.mult).then_inc(nt_ok, 1)
                    ve.wait_ge(nt_ok, m + k + 1)
                    if k >= 2:
                        ve.wait_ge(h_ok, m + k - 1)
                    for b, a, e in kinds:
                        i = ve.tensor_scalar(n32[:, k % 2, a:e], nt[:, k % 2, a:e], wsc[:, k, b:b + 1], wsh[:, k, b:b + 1],
                                             ALU.mult, ALU.add)
                    i.then_inc(n32_ok, 1)
                    if k:
                        lo(k - 1)
                lo(KC - 1)

            def residual(k, up, banks, t0):
                kinds = [(0, 0, TC), (1, TC, T)][t0 // TC:]
                for m in range(2):
                    for b, a, e in kinds:
                        xs = x[:, bass.ds(k + m, 1), a:e]
                        g = gcol[:, :, b]
                        i = ve.scalar_tensor_tensor(xs, banks[m][:, None, a:e], g[:, bass.ds(k + m, 1)], xs, ALU.mult, ALU.add)
                    i.then_inc(xup, 1)

            for s, n in [(lo_done, LO), (conv_ok, 2), (o_free[0], 1), (o_free[1], 1), (y_ok, 1), (a_free, 1), (a32_ok, 2),
                         (al_ok, 2), (qkr_ok, 1), (w_ok, 2), (xup, 4)]:
                ve.sem_inc(s, n)
            ve.memset(eps, EPS).then_inc(eps_ok, 1)
            ve.wait_ge(sqd, 1)
            ve.tensor_copy(ssq[:, :], sq[:, 0, :]).then_inc(ssd, 1)
            for k in range(1, KC):
                add_square(k, 0, k % 2)
            inverse(0, 0)
            ve.wait_ge(a0_mm, 1)
            step(ve.tensor_tensor(adac[:, 0, 0:16, :], AB[:, 0:32].rearrange("p (c b) -> p c b", b=2),
                                  cc("bada", 0, 16)[:, :, None].to_broadcast([P, 16, 2]), ALU.add))
            columns(0, cc("n1w", 0, KC), 0)
            ve.wait_ge(dth_ok, 1)
            ve.scalar_tensor_tensor(dtl, dtraw, WS, dth, ALU.mult, ALU.subtract).then_inc(dtl_ok, 1)
            cvt(Unit(U_SSD0), 1024)
            h_lo(0, 0)
            cvt(Unit(U_SSD0 + 1), 1024)

            ve.wait_ge(dt_mm, 1)
            db = cc("dtb")
            ve.scalar_tensor_tensor(dx.rearrange("p (c h) -> p c h", c=NCH), OB[0][:, 0:256].rearrange("p (c h) -> p c h", c=NCH),
                                    1.0 / (WS * AS), db[:, None, :].to_broadcast([P, NCH, 64]), ALU.mult, ALU.add).then_inc(dtv, 1)
            ve.wait_ge(dta, 2)
            step(ve.tensor_scalar(dr, de, 2.0, None, ALU.add))
            step(ve.reciprocal(dr, dr))
            step(ve.tensor_tensor(dz, de, dr, ALU.mult))
            step(ve.tensor_tensor(dz2, dz, dz, ALU.mult))
            step(ve.tensor_scalar(dq, dz2, 1.0 / 17.0, None, ALU.mult))
            for k in (15, 13, 11, 9, 7, 5, 3):
                step(ve.scalar_tensor_tensor(dq, dq, 1.0 / k, dz2, ALU.add, ALU.mult))
            step(ve.scalar_tensor_tensor(dq, dq, 1.0, dz, ALU.add, ALU.mult))
            step(ve.tensor_scalar(dr, dx, 0.0, None, ALU.max))
            dtf = PR[:, DT].rearrange("p c h -> p (c h)")
            step(ve.scalar_tensor_tensor(dtf, dq, 2.0, dr, ALU.mult, ALU.add))
            ve.wait_ge(dta, 3)
            step(ve.tensor_scalar(da, da, -DS, None, ALU.mult))
            step(ve.tensor_tensor(dr.rearrange("p (c h) -> p c h", c=NCH), dtf.rearrange("p (c h) -> p c h", c=NCH),
                                  da[:, None, :].to_broadcast([P, NCH, 64]), ALU.mult))
            step(ve.tensor_copy(adh, dr))
            ve.tensor_tensor(adl, dr, adh, ALU.subtract).then_inc(adt_ok, 1)

            def conv_tile(g, tile):
                n = g * 6 + tile
                base = g * 36 + tile * 6
                cw = cc("conv")
                ac = acc.rearrange("p (s t) -> p s t", s=2)
                ve.wait_ge(pre_ok, n + 1)
                if not (isinstance(g, int) and tile == 0):
                    ve.wait_ge(xbc_ok, n)
                ve.tensor_scalar(ac, pre[:, tile % 2, :, 0:TC], cw[:, bass.ds(base, 1)], cw[:, bass.ds(base + 5, 1)],
                                 ALU.mult, ALU.add).then_inc(conv, 1)
                for j in range(1, 5):
                    ve.wait_ge(conv, n * 4 + j)
                    ve.scalar_tensor_tensor(ac, pre[:, tile % 2, :, j:j + TC], cw[:, bass.ds(base + j, 1)], ac, ALU.mult,
                                            ALU.add).then_inc(conv if j < 4 else conv_ok, 1)

            def wide(b):
                return b[:, :].rearrange("p (h f) -> p h f", h=HG)

            def per_head(q, c, d):
                a = PRg[:, q, 2 * c + d, :]
                return a[:, :, None].to_broadcast([P, HG, HP])

            def chunk(g, c, between=None):
                if c == 0:
                    ve.wait_ge(o_free[1], g * O_PER + (O_CB[1] + 2))
                for q in range(4):
                    ve.wait_ge(e_ok, g * 16 + (4 * c + q + 3))
                    ve.tensor_tensor(E[:, q % 2], E[:, q % 2], cb[:, c, None, :].to_broadcast([P, 4, P]), ALU.mult).then_inc(t_ok, 1)
                    if between and q in between:
                        between[q]()
                parts = []
                for d in sorted(YOFF[c]):
                    f = YOFF[c][d][1]
                    dst = (ya, yb)[d]
                    ve.wait_ge(o_mm[d], g * O_PER + (f + 1))
                    ve.tensor_tensor(dst.rearrange("p (h f) -> p h f", h=HG), wide(OB[d]), per_head(DOUT, c, d), ALU.mult).then_inc(o_free[d], 1)
                    ve.wait_ge(o_free[d], g * O_PER + (f + 2))
                    parts.append(dst)
                if len(parts) == 2:
                    ve.tensor_tensor(ya, ya, yb, ALU.add).then_inc(yp, 1)
                    ve.wait_ge(yp, g * 2 + (c - 1))
                ve.wait_ge(yd, g * 16 + (4 * c + 6))
                ve.tensor_tensor(ys[:, c % 2, :], parts[0], YB[:, :], ALU.add).then_inc(y_ok, 1)

            def skip(g, c):
                ve.wait_ge(xD_ok, g * QT + QT)
                ve.wait_ge(a_mm, g * A_PER + (A_YT[c] + 3))
                ve.wait_ge(g_ok, g * NCH + (c + 1))
                ve.tensor_tensor(gt[:, c % 2, :].rearrange("p (q l) -> p q l", q=QT), AB[:, :].rearrange("p (q l) -> p q l", q=QT),
                                 xD[:, :, c * P:(c + 1) * P], ALU.add).then_inc(a_free, 1)

            def group(g, u, more):
                PRf = PR.rearrange("p q c h -> p (q c) h")
                ve.tensor_copy(PRg.rearrange("p q c h -> p (q c) h"), PRf[:, :, bass.ds(g * HG, HG)]).then_inc(prg_ok, 1)
                ve.tensor_copy(adgh.rearrange("p (c h) -> p c h", c=8), adh.rearrange("p (c h) -> p c h", c=8)[:, :, bass.ds(g * HG, HG)]).then_inc(prg_ok, 1)
                ve.tensor_copy(adgl.rearrange("p (c h) -> p c h", c=8), adl.rearrange("p (c h) -> p c h", c=8)[:, :, bass.ds(g * HG, HG)]).then_inc(prg_ok, 1)
                ve.tensor_copy(dg, cc("dskip")[:, bass.ds(g * QT, QT)]).then_inc(prg_ok, 1)
                cvt(u.plus(1))
                ve.wait_ge(prg_ok, g * 4 + 4)
                for c in range(NCH):
                    b, f = O_XT[c]
                    ve.wait_ge(o_mm[b], g * O_PER + (f + 1))
                    for d in range(2):
                        i = ve.tensor_tensor(xd[:, c, d, :].rearrange("p (h f) -> p h f", h=HG), wide(OB[b]), per_head(DT, c, d), ALU.mult)
                    i.then_inc(o_free[b], 1)
                cvt(u.plus(2), 1024 if more else UF)
                for k in range(2, 6):
                    b, f = O_ST[k]
                    ve.wait_ge(o_mm[b], g * O_PER + (f + 1))
                    ve.wait_ge(hm_ok, g * 4 + (k - 1))
                    ve.tensor_tensor(Hs[:, k, :], Hs[:, k, :], OB[b][:, :], ALU.add).then_inc(o_free[b], 1)
                ada_out(g + ADA_FIRST, g * A_PER + A_ADA)
                if more:
                    cvt(u.plus(3), 1024)
                chunk(g, 0)
                if more:
                    cvt(u.plus(4))
                chunk(g, 1, {1: lambda: conv_tile(g + 1, 0)} if more else None)
                skip(g, 0)
                if more:
                    cvt(u.plus(5))
                chunk(g, 2, {1: lambda: conv_tile(g + 1, 1)} if more else None)
                skip(g, 1)
                if more:
                    cvt(u.plus(6))
                chunk(g, 3, {0: lambda: conv_tile(g + 1, 2), 2: lambda: conv_tile(g + 1, 3)} if more else None)
                skip(g, 2)
                skip(g, 3)
                if more:
                    conv_tile(g + 1, 4)
                    conv_tile(g + 1, 5)

            u = Unit(U_SSD0)
            conv_tile(0, 0)
            cvt(u.plus(2))
            conv_tile(0, 1)
            cvt(u.plus(3))
            conv_tile(0, 2)
            conv_tile(0, 3)
            ve.wait_ge(A_mm, 1)
            ve.wait_ge(aexp, 2)
            nega = PR[:, NEGA].rearrange("p c h -> p (c h)")
            ve.tensor_scalar(nega, OB[1][:, 0:256], -1.0 / DS, None, ALU.mult).then_inc(pr_ok, 1)
            ve.wait_ge(pr_ok, 1)
            ve.scalar_tensor_tensor(PR[:, DST].rearrange("p c h -> p (c h)"), OB[1][:, 256:512], 1.0 / DS, nega, ALU.mult, ALU.add).then_inc(pr_ok, 1)
            cvt(u.plus(4))
            conv_tile(0, 4)
            conv_tile(0, 5)
            ve.wait_ge(aexp, 3)
            with ve.Fori(0, NG - 1) as g:
                group(g, Unit(U_GRP, 6, g), True)
            group(NG - 1, Unit(U_TAIL), False)

            cvt_half(Unit(U_OUT + 1), 0, 0, UF // 2)
            inverse(1, 0)
            gw = small[:, 16:32]
            step(ve.tensor_scalar(gw, cc("gnw"), AS, None, ALU.mult))
            ve.wait_ge(a_free, 1 + 4 * A_PER)
            gates(0, 16, WS * AS)
            step(ve.memset(ssq[:, :], 0.0))
            ve.wait_ge(c_bc, 2)
            for k in range(17):
                if k < 16:
                    if k >= 2:
                        ve.wait_ge(gn_ok, k - 1)
                    ve.scalar_tensor_tensor(nt[:, k % 2, :], G[:, k, :], gw[:, k:k + 1], OB[1][:, :], ALU.mult, ALU.mult).then_inc(gn_t, 1)
                if k:
                    ve.wait_ge(gn_h, k)
                    ve.tensor_tensor(gl[:, k - 1, :], nt[:, (k - 1) % 2, :], gh[:, k - 1, :], ALU.subtract).then_inc(gn_ok, 1)

            def sums(n, t0):
                for m in range(2):
                    add_square(n + m, t0, m)

            ve.wait_ge(srow_ok, 1)
            with ve.Fori(0, 2) as i:
                for m in range(2):
                    u = Unit(U_OUT + 2 * m, 4, i)
                    for k in range(2):
                        ada_unit(i * 4 + (2 * m + k), k)
                        cvt_on(u.plus(k + 1))
                    ve.wait_ge(unit_done, u.half + (UD + 4))
                    residual(i * 4 + 2 * m, None, GB[2 * m:2 * m + 2], 0)
                    sums(i * 4 + (SQ_X[2] + 2 * m), 0)

            def ffn(layer, ugu, udn, t0, with_ada):
                n0 = layer * FC
                with ve.Fori(0, FC // 2) as i:
                    u = Unit(ugu, 2, i)
                    for k in range(2):
                        if with_ada:
                            ada_unit(i * 2 + (ADA_OUT + k), k)
                        cvt_on(u.plus(k + 1))
                    ve.wait_ge(unit_done, u.half + (UD + 4))
                    for m in range(2):
                        ve.wait_ge(sg_ok, i * 2 + (n0 + m + 3))
                        ve.wait_ge(al_ok, i * 2 + (n0 + m + 1))
                        ve.scalar_tensor_tensor(a32[:, m, t0:T], GB[2 + m][:, t0:T], FS / (WS * AS), sg[:, m, t0:T], ALU.mult,
                                                ALU.mult).then_inc(a32_ok, 1)
                    for m in range(2):
                        ve.wait_ge(ah_ok, i * 2 + (n0 + m + 1))
                        am = bass.ds(i * 2 + m, 1)
                        ve.tensor_tensor(al[:, am, t0:T], a32[:, m, None, t0:T], ah[:, am, t0:T], ALU.subtract).then_inc(al_ok, 1)
                if with_ada:
                    ve.wait_ge(ada_ok, ADA_OUT + ADA_GU)
                gates(layer, 40, WS * FS)
                step(ve.memset(ssq[:, :], 0.0))
                for m in range(4):
                    for k in range(3):
                        if with_ada and m < 3 and k < 2:
                            ada_unit(ADA_OUT + ADA_GU + 2 * m + k, k)
                        nxt = Unit(udn + 3 * m + k + 1)
                        if nxt.base < U_DN1 + 12:
                            a, b = DNK[(k + 1) % 3]
                            cvt_on(nxt, UF if 3 * m + k + 1 == 12 else (b - a) * UN)
                    ve.wait_ge(unit_done, 2 * (udn + 3 * m + 3) + UD)
                    residual(2 * m, None, GB[2 * (m % 2):2 * (m % 2) + 2], t0)
                    sums(SQ_X[3 + 2 * layer] + 2 * m, t0)

            ve.wait_ge(ada_ok, ADA_OUT)
            columns(0, cc("n2w", 0, KC), 24)
            inverse(2, 0)
            h_lo(2, 0)
            ffn(0, U_GU0, U_DN0, 0, True)

            ve.wait_ge(ada_ok, 48 - ADA_PE)
            columns(1, cc("n1w", KC, 2 * KC), 0)
            gates(1, 16, WS * AS)
            inverse(3, 0)
            h_lo(3, 0)
            lq = cc("lqk").rearrange("p (s a d) -> p s a d", s=2, a=2)
            ve.tensor_tensor(lp, lq[:, 0], lq[:, 1], ALU.mult).then_inc(lam, 1)
            ve.wait_ge(lam, 1)
            ve.tensor_reduce(ls, lp, AXX, ALU.add).then_inc(lam, 1)
            ve.wait_ge(lam, 3)
            ve.scalar_tensor_tensor(nlam, ls[:, 1:2], LAMBDA_INIT, ls[:, 0:1], ALU.subtract, ALU.subtract).then_inc(lam, 1)
            sub = small[:, 8:9]
            step(ve.tensor_scalar(sub, cc("subln"), AS * (1.0 - LAMBDA_INIT), None, ALU.mult))
            step(ve.memset(ssq[:, :], 0.0))
            with ve.Fori(0, 2) as i:
                cvt_on(Unit(U_V + 1, 2, i))
                cvt_on(Unit(U_V + 2, 2, i))

            def turn(i):
                lat = kst[:, :, TC:T]
                for n, (src, b, dst) in enumerate([(qst, AB, qr), (lat, YB, kr[:, :, TC:T])]):
                    ve.wait_ge(rot_mm, i * 2 + (n + 1))
                    ve.tensor_tensor(r1, b[:, :].rearrange("p (h t) -> p h t", h=2), sinT[:, None, :].to_broadcast([P, 2, TC]), ALU.mult).then_inc(rope, 1)
                    ve.tensor_tensor(r2, src, cosT[:, None, :].to_broadcast([P, 2, TC]), ALU.mult).then_inc(rope, 1)
                    ve.wait_ge(rope, i * 6 + (3 * n + 2))
                    ve.tensor_tensor(dst, r1, r2, ALU.add).then_inc(rope, 1)
                    ve.wait_ge(rope, i * 6 + (3 * n + 3))
                ve.tensor_copy(kr[:, :, 0:TC], kst[:, :, 0:TC]).then_inc(qkr_ok, 1)

            def maxima(i, n):
                N = i * 4 + n
                ve.wait_ge(s_mm, N + 1)
                for m in range(2):
                    ve.tensor_reduce(mx[:, n % 2, m:m + 1], SB[n % 2][m][:, :], AXX, ALU.max).then_inc(mx_ok, 1)
                ve.wait_ge(mx_ok, N * 2 + 2)
                ve.tensor_scalar(nb[:, n % 2, :], mx[:, n % 2, :], -0.125, None, ALU.mult).then_inc(nb_ok, 1)

            def weigh(i, n):
                N, b = i * 4 + n, n % 2
                ve.wait_ge(ea_ok, N + 3)
                ve.reciprocal(rs[:, b, :], es[:, b, :]).then_inc(rs_ok, 1)
                ve.wait_ge(rs_ok, N * 2 + 1)
                ve.tensor_scalar(rs[:, b, 1:2], rs[:, b, 1:2], nlam, None, ALU.mult).then_inc(rs_ok, 1)
                ve.wait_ge(rs_ok, N * 2 + 2)
                ve.tensor_scalar(EA[:, b, 1, :], EA[:, b, 1, :], rs[:, b, 1:2], None, ALU.mult).then_inc(w_t, 1)
                ve.wait_ge(w_t, N + 1)
                ve.wait_ge(wt_mm, N + 1)
                ve.scalar_tensor_tensor(wmt[:, b, :], EA[:, b, 0, :], rs[:, b, 0:1], EA[:, b, 1, :], ALU.mult, ALU.add).then_inc(w_ok, 1)

            ve.wait_ge(lam, 4)
            cvt_on(Unit(U_QK + 1))
            cvt_on(Unit(U_QK + 2))
            turn(0)
            with ve.Fori(1, 4) as i:
                u = Unit(U_QK, 2, i)
                j = i - 1
                cvt_on(u.plus(1))
                maxima(j, 0)
                maxima(j, 1)
                weigh(j, 0)
                maxima(j, 2)
                weigh(j, 1)
                cvt_on(u.plus(2))
                maxima(j, 3)
                weigh(j, 2)
                weigh(j, 3)
                turn(i)
            maxima(3, 0)
            for n in range(4):
                if n < 3:
                    maxima(3, n + 1)
                weigh(3, n)
            ve.wait_ge(ort_s, 1)
            ve.reciprocal(ort.rearrange("p b h -> p (b h)"), ort.rearrange("p b h -> p (b h)")).then_inc(ort_ok, 1)
            ve.wait_ge(ort_ok, 1)
            for b in range(2):
                ve.tensor_tensor(osb[:, b], osb[:, b], ort[:, b, :][:, :, None].to_broadcast([P, AHEADS, P]), ALU.mult).then_inc(on_ok, 1)
            for j in range(5):
                if j < 4:
                    ve.wait_ge(ot_mm, j + 1)
                    if j >= 2:
                        ve.wait_ge(o_ok, j - 1)
                    ve.tensor_scalar(o32[:, j % 2, :], OTB[j][:, :], sub, None, ALU.mult).then_inc(o32_ok, 1)
                if j:
                    hq, qb = (j - 1) // 2, (j - 1) % 2
                    ve.wait_ge(oh_ok, j)
                    part = (slice(None), slice(4 * hq, 4 * hq + 4), slice(qb * P, (qb + 1) * P))
                    ve.tensor_tensor(ol[part], o32[:, (j - 1) % 2, :].rearrange("p (h t) -> p h t", h=4), oh[part], ALU.subtract).then_inc(o_ok, 1)
            with ve.Fori(0, 2) as i:
                for m in range(2):
                    cvt_on(Unit(U_WO + m + 1, 2, i))
                    ve.wait_ge(unit_done, i * 4 + (2 * (U_WO + m) + UD + 2))
                    residual(i * 4 + 2 * m, None, GB[2 * m:2 * m + 2], TC)
                    sums(i * 4 + (SQ_X[4] + 2 * m), TC)
            columns(1, cc("n2w", KC, 2 * KC), 24)
            inverse(4, 2)
            h_lo(4, TC)
            ffn(1, U_GU1, U_DN1, TC, False)
            inverse(5, 2)
            ve.wait_ge(c_bc, 6)
            fw = cc("fnw")
            for k in range(KC):
                ve.scalar_tensor_tensor(fin[:, k, :], x[:, k, TC:T], fw[:, k:k + 1], OB[1][:, TC:T], ALU.mult, ALU.mult).then_inc(fin_ok, 1)

        @block.gpsimd
        def _(po):
            po.sem_inc(g_ok, 2)
            po.wait_ge(a0_mm, 1)
            po.memset(pre[:, 0], 0.0).then_inc(pads_ok, 1)
            po.memset(pre[:, 1], 0.0).then_inc(pads_ok, 1)
            po.wait_ge(c_ss, 1)
            po.memset(ssq[:, :], 0.0).then_inc(pads_ok, 1)
            po.wait_ge(pads_ok, 3)

            def group(g):
                po.wait_ge(xbc_ok, g * 6 + 6)
                po.wait_ge(prg_ok, g * 4 + 4)

                def summand(k):
                    c, d = ST[k]
                    b, f = O_XT[c]
                    po.wait_ge(o_free[b], g * O_PER + (f + 2))
                    sb_, sf = O_ST[k]
                    if k >= 2:
                        po.wait_ge(o_mm[sb_], g * O_PER + sf)
                    w = PRg[:, DST, 2 * c + d, :]
                    po.tensor_tensor(xdd[:, k % 2, :].rearrange("p (h f) -> p h f", h=HG), xd[:, c, d, :].rearrange("p (h f) -> p h f", h=HG),
                                     w[:, :, None].to_broadcast([P, HG, HP]), ALU.mult).then_inc(xdd_ok, 1)

                def decay(k):
                    c, d = ST[k]
                    frm = ST_FROM[k]
                    b, f = O_ST[frm]
                    po.wait_ge(o_free[b], g * O_PER + (f + 2))
                    w = PRg[:, DCH, 2 * c + d, :]
                    po.tensor_tensor(Hs[:, k, :].rearrange("p (h f) -> p h f", h=HG), Hs[:, frm, :].rearrange("p (h f) -> p h f", h=HG),
                                     w[:, :, None].to_broadcast([P, HG, HP]), ALU.mult).then_inc(hm_ok, 1)

                summand(0)
                for q in range(QT):
                    po.tensor_scalar(xD[:, q, :], xbc[:, 2 + q, :], dg[:, q:q + 1], 0.0, ALU.mult, ALU.add).then_inc(xD_ok, 1)
                summand(1)
                summand(2)
                summand(3)
                decay(2)
                decay(3)
                summand(4)
                decay(4)
                summand(5)
                decay(5)
                for c in range(NCH):
                    if c == 0:
                        po.wait_ge(zs_ok, g * QT + QT)
                    po.wait_ge(a_free, g * A_PER + (A_YT[c] + 2))
                    gs = G[:, bass.ds(g * QT, QT), c * P:(c + 1) * P]
                    po.tensor_tensor(gs, gs, gt[:, c % 2, :].rearrange("p (q l) -> p q l", q=QT), ALU.mult).then_inc(g_ok, 1)
                for q in range(QT):
                    n = g * QT + (SQ_G + q)
                    po.wait_ge(sqd, n + 1)
                    po.wait_ge(ssd, n)
                    po.tensor_tensor(ssq[:, :], ssq[:, :], sq[:, q % 2, :], ALU.add).then_inc(ssd, 1)

            with po.Fori(0, NG) as g:
                group(g)

            po.wait_ge(y_ok, NG * NCH + 1)
            for b in range(2):
                po.dma_start(abuf[:, b], wadaT[b]).then_inc(abuf_in[b], 16)
            with po.Fori(0, (48 - ADA_PE) // 2 - 1) as i:
                for b in range(2):
                    po.wait_ge(ada_sum, i * 2 + (b + 1))
                    po.dma_start(abuf[:, b], wadaT[i * 2 + (b + 2)]).then_inc(abuf_in[b], 16)

        @block.tensor
        def _(pe):
            def gemm(u, outs, acts, ks, first, last, width=UN, hooks=None, t0=0, t1=T, ready=None, swap=False):
                ahi, alo = acts
                for j, k in enumerate(ks):
                    if j % 4 == 0:
                        pe.wait_ge(lo_done, u.half + (LO + 1 + j // 4))
                    if ready is not None:
                        pe.wait_ge(ready[0], ready[1] + j + 1)
                    for m, o in outs:
                        wsl = slice(j * width + m * P, j * width + (m + 1) * P)
                        st = k == first
                        en = k == last
                        pe.matmul(o, wh[:, u.slot, wsl], ahi[:, k, t0:t1], start=st, stop=False)
                        pe.matmul(o, wh[:, u.slot, wsl], alo[:, k, t0:t1], start=False, stop=False)
                        i = pe.matmul(o, wl[:, u.slot, wsl], ahi[:, k, t0:t1], start=False, stop=en)
                    if j in (3, len(ks) - 1):
                        i.then_inc(unit_done, 1)
                    if hooks and j in hooks:
                        hooks[j]()

            H = (hh, hl)

            def ssum(n, cs):
                for c in range(cs, 4):
                    i = pe.matmul(OB[0][:, c:c + 1], ssq[:, c * P:(c + 1) * P], ones[:, 0:1], start=True, stop=True)
                i.then_inc(c_ss, 1)

            def bcast(n, cs):
                pe.wait_ge(c_dg, n + 1)
                pe.matmul(OB[1][:, cs * P:T], ones, rdg[:, cs * P:T], start=True, stop=True).then_inc(c_bc, 1)

            def ada(turn, fill):
                pe.wait_ge(araw_in, turn * 16 + 16)
                pe.wait_ge(a_free, fill + 1)
                for m in range(2):
                    for k in range(KC):
                        i = pe.matmul(AB[:, 2 * m:2 * m + 2], araw[:, k * UN + m * P:k * UN + (m + 1) * P], s2[:, k, :],
                                      start=(k == 0), stop=(k == KC - 1))
                i.then_inc(a_mm, 1)

            for s, n in [(unit_done, UD), (yd, 2), (a_mm, 2), (wt_mm, 2)]:
                pe.sem_inc(s, n)
            pe.wait_ge(s2_ok, 1)
            for b in range(4):
                pe.wait_ge(in_ada[b], 16)
                for a in (2 * b, 2 * b + 1):
                    for m in range(2):
                        o = 2 * (2 * a + m)
                        for k in range(KC):
                            i = pe.matmul(AB[:, o:o + 2], afirst[:, a, k * UN + m * P:k * UN + (m + 1) * P], s2[:, k, :],
                                          start=(k == 0), stop=(k == KC - 1))
                if b == 1:
                    pe.wait_ge(in_kp, 16)
                    pe.wait_ge(ssd, KC)
                    ssum(0, 0)
            i.then_inc(a0_mm, 1)
            bcast(0, 0)

            u = Unit(U_SSD0)
            gemm(u, [(0, GB[0][:, :])], H, range(KC), 0, KC - 1, width=P, ready=(h_ok, 0))
            pe.wait_ge(dtl_ok, 1)
            pe.wait_ge(c_rt, 1)
            for c in range(NCH):
                tk = slice(c * P, (c + 1) * P)
                for k in range(KC):
                    o, w_ = OB[0][:, c * 64:(c + 1) * 64], slice(k * 64, (k + 1) * 64)
                    pe.matmul(o, hh[:, k, tk], dth[:, w_], start=(k == 0), stop=False)
                    pe.matmul(o, hl[:, k, tk], dth[:, w_], start=False, stop=False)
                    i = pe.matmul(o, hh[:, k, tk], dtl[:, w_], start=False, stop=(k == KC - 1))
            i.then_inc(dt_mm, 1)
            gemm(u.plus(1), [(0, GB[1][:, :])], H, range(KC), 0, KC - 1, width=P)
            pe.wait_ge(pre_ok, 2)
            gemm(u.plus(2), [(0, GB[0][:, :]), (1, GB[1][:, :])], H, range(KC), 0, KC - 1)
            pe.wait_ge(masks_ok, 4)
            pe.wait_ge(adt_ok, 1)
            for j, mask in enumerate((masks[:, 0, :], masks[:, 1, :])):
                a8 = slice(32 * j, 32 * j + 32)
                o = OB[1][:, 0:256].rearrange("p (c h) -> p c h", c=NCH)[:, :, a8]
                for n, half in enumerate((adh, adl)):
                    pe.matmul(o, mask, half.rearrange("p (c h) -> p c h", c=NCH)[:, :, a8], start=(n == 0), stop=(n == 1))
            for n, half in enumerate((adh, adl)):
                i = pe.matmul(OB[1][:, 256:512], masks[:, 2, :], half, start=(n == 0), stop=(n == 1))
            i.then_inc(A_mm, 1)
            pe.wait_ge(pre_ok, 4)
            gemm(u.plus(3), [(0, GB[0][:, :]), (1, GB[1][:, :])], H, range(KC), 0, KC - 1)
            pe.wait_ge(dtv, 1)
            pe.wait_ge(aexp, 2)
            pe.wait_ge(pr_ok, 2)

            def group(g, u, more):
                def o_turn(b, f):
                    pe.wait_ge(o_free[b], g * O_PER + (f + 1))

                def x_turn(c):
                    b, f = O_XT[c]
                    if c == 0:
                        pe.wait_ge(xbc_ok, g * 6 + 6)
                    o_turn(b, f)
                    for q in range(QT):
                        i = pe.transpose(OB[b][:, q * P:(q + 1) * P], xbc[:, 2 + q, c * P:(c + 1) * P], ident)
                    i.then_inc(o_mm[b], 1)

                def b_turn():
                    o_turn(*O_B)
                    for c in range(NCH):
                        i = pe.transpose(OB[0][:, c * P:(c + 1) * P], xbc[:, 0, c * P:(c + 1) * P], ident)
                    i.then_inc(o_mm[0], 1)

                def cb_mm():
                    o_turn(*O_CB)
                    for c in range(NCH):
                        cs = slice(c * P, (c + 1) * P)
                        i = pe.matmul(OB[1][:, cs], xbc[:, 0, cs], xbc[:, 1, cs], start=True, stop=True)
                    i.then_inc(o_mm[1], 1)

                def state(k):
                    c, d = ST[k]
                    b, f = O_ST[k]
                    if k == 0:
                        pe.wait_ge(o_free[0], g * O_PER + (O_B[1] + 2))
                    pe.wait_ge(xdd_ok, g * 6 + (k + 1))
                    o_turn(b, f)
                    pe.matmul(OB[b][:, :], Bt[:, c * P:(c + 1) * P], xdd[:, k % 2, :], start=True, stop=True).then_inc(o_mm[b], 1)

                def exponents(c, q):
                    d, hq = q % 2, q // 2
                    n = g * 16 + (4 * c + q)
                    pe.wait_ge(e_ok, n + 1)
                    if c == 0 and q == 0:
                        pe.wait_ge(prg_ok, g * 4 + 3)
                    o = DB[q % 2]
                    pe.matmul(o[:, :].rearrange("p (h l) -> p h l", h=4), idb[:, :], negm[:, d, None, :].to_broadcast([P, 4, P]), start=True, stop=False,
                              skip_group_check=True)
                    for h in range(4):
                        hc = (2 * c + d) * HG + 4 * hq + h
                        for m, half in enumerate((adgh, adgl)):
                            i = pe.matmul(o[:, h * P:(h + 1) * P], half[:, hc:hc + 1].to_broadcast([P, P]), masks[:, d, :],
                                          start=False, stop=(m == 1), skip_group_check=True)
                    i.then_inc(d_mm, 1)

                def within(c, q):
                    d, hq = q % 2, q // 2
                    pe.wait_ge(t_ok, g * 16 + (4 * c + q + 1))
                    if q == 0:
                        pe.wait_ge(y_ok, g * NCH + (c + 1))
                    for h in range(4):
                        hs = slice((4 * hq + h) * HP, (4 * hq + h + 1) * HP)
                        i = pe.matmul(YB[:, hs], E[:, q % 2, h, :], xd[:, c, d, hs], start=(q == 0 and h == 0), stop=(q % 2 == 1),
                                      skip_group_check=True)
                    i.then_inc(yd, 1)

                def from_states(c):
                    for d in sorted(YOFF[c]):
                        k, f = YOFF[c][d]
                        sb_, sf = O_ST[k]
                        pe.wait_ge(o_free[sb_], g * O_PER + (sf + 2))
                        if c == 0:
                            pe.wait_ge(bt_ok, g + 1)
                        o_turn(d, f)
                        pe.matmul(OB[d][:, :], Cc[:, c * P:(c + 1) * P], Hs[:, k, :], start=True, stop=True).then_inc(o_mm[d], 1)

                def y_turn(c):
                    pe.wait_ge(y_ok, g * NCH + (c + 2))
                    pe.wait_ge(a_free, g * A_PER + (A_YT[c] + 1))
                    for q in range(QT):
                        i = pe.transpose(AB[:, q * P:(q + 1) * P], ys[:, c % 2, q * P:(q + 1) * P], ident)
                    i.then_inc(a_mm, 1)

                def scan(c, tail=None):
                    def first():
                        exponents(c, 0)
                        exponents(c, 1)
                        from_states(c)

                    def second():
                        within(c, 0)
                        exponents(c, 2)

                    def third():
                        within(c, 1)
                        exponents(c, 3)
                        if tail:
                            tail()

                    def fourth():
                        within(c, 2)

                    def fifth():
                        within(c, 3)

                    return {0: first, 2: second, 4: third, 6: fourth, 7: fifth}

                def unit(k, outs, hooks, width=UN):
                    gemm(u.plus(k), outs, H, range(KC), 0, KC - 1, width=width, hooks=hooks)

                both = [(0, GB[0][:, :]), (1, GB[1][:, :])]
                pe.wait_ge(pre_ok, g * 6 + 6)
                unit(0, both, {1: lambda: (x_turn(0), x_turn(1)), 3: lambda: (x_turn(2), x_turn(3)), 5: b_turn, 6: cb_mm})
                pe.wait_ge(zs_ok, g * QT + 2)
                unit(1, both, {1: lambda: state(0), 2: lambda: state(1), 3: lambda: state(2), 4: lambda: state(3),
                               6: lambda: state(4), 7: lambda: state(5)})
                ada(g, g * A_PER + A_ADA)
                pe.wait_ge(zs_ok, g * QT + 4)
                for c in range(4):
                    hooks = scan(c, (lambda: y_turn(c - 1)) if c else None)
                    if more:
                        if c < 2:
                            unit(2 + c, [(0, GB[c][:, :])], hooks, P)
                        else:
                            pe.wait_ge(pre_ok, g * 6 + (8 if c == 2 else 10))
                            unit(2 + c, both, hooks)
                    else:
                        for k in sorted(hooks):
                            hooks[k]()
                y_turn(3)

            with pe.Fori(0, NG - 1) as g:
                group(g, Unit(U_GRP, 6, g), True)
            group(NG - 1, Unit(U_TAIL), False)

            pe.wait_ge(ssd, SQ_G + 16)
            ssum(1, 0)
            bcast(1, 0)
            with pe.Fori(0, 2) as i:
                for m in range(2):
                    banks = [(j, GB[2 * m + j][:, :]) for j in range(2)]
                    pe.wait_ge(e_ok, 66)
                    pe.wait_ge(xup, i * 4 + (2 * m + 2))
                    for hf in range(2):
                        gemm(Unit(U_OUT + 2 * m + hf, 4, i), banks, (gh, gl), range(8 * hf, 8 * hf + 8), 0, 15,
                             ready=(gn_ok, 8 * hf))

            def ffn(layer, ugu, udn, t0, h0):
                n0 = layer * FC
                with pe.Fori(0, FC // 2) as i:
                    u = Unit(ugu, 2, i)
                    for s in range(2):
                        if s == 0:
                            pe.wait_ge(sg_ok, i * 2 + (n0 + 2))
                        else:
                            pe.wait_ge(a32_ok, i * 2 + (n0 + 2))
                        banks = [(j, GB[2 * s + j][:, t0:T]) for j in range(2)]
                        gemm(u.plus(s), banks, H, range(KC), 0, KC - 1, t0=t0, ready=(h_ok, h0) if s == 0 else None)
                pe.wait_ge(a32_ok, n0 + FC + 2)
                for m in range(4):
                    banks = [(j, GB[2 * (m % 2) + j][:, t0:T]) for j in range(2)]
                    if m >= 2:
                        pe.wait_ge(xup, 12 + 16 * layer + 2 * (m - 1))
                    for k, (a, b) in enumerate(DNK):
                        gemm(Unit(udn + 3 * m + k), banks, (ah, al), range(a, b), 0, FC - 1, t0=t0,
                             ready=(al_ok, 2 + n0 + a) if m == 0 else None)

            def norm(n, cs, sums):
                pe.wait_ge(ssd, sums)
                ssum(n, cs)
                bcast(n, cs)

            norm(2, 0, SQ_X[3])
            ffn(0, U_GU0, U_DN0, 0, KC)

            norm(3, 0, SQ_X[4])
            with pe.Fori(0, 2) as i:
                for s in range(2):
                    u = Unit(U_V + s, 2, i)
                    for k in range(KC):
                        if k % 4 == 0:
                            pe.wait_ge(lo_done, u.half + (LO + 1 + k // 4))
                        if s == 0:
                            pe.wait_ge(h_ok, 2 * KC + k + 1)
                        w_ = slice(k * UN, (k + 1) * UN)
                        for c in range(4):
                            if s == 0 and k == 0:
                                pe.wait_ge(v_ok, i * 4 + (c + 1))
                            o, tk = GB[c][:, s * UN:(s + 1) * UN], slice(c * P, (c + 1) * P)
                            pe.matmul(o, hh[:, k, tk], wh[:, u.slot, w_], start=(k == 0), stop=False)
                            pe.matmul(o, hl[:, k, tk], wh[:, u.slot, w_], start=False, stop=False)
                            j = pe.matmul(o, hh[:, k, tk], wl[:, u.slot, w_], start=False, stop=(k == KC - 1))
                        if k % 4 == 3:
                            j.then_inc(unit_done, 1)

            def scores(i, n):
                hd, qb = n // 2, n % 2
                if n == 0:
                    pe.wait_ge(qkr_ok, i + 2)
                pe.wait_ge(ea_ok, i * 4 + (n + 1))
                for m in range(2):
                    rows = slice(m * HP, (m + 1) * HP)
                    j = pe.matmul(SB[n % 2][m][:, :], qr[rows, hd, qb * P:(qb + 1) * P], kr[rows, hd, :], start=True, stop=True)
                j.then_inc(s_mm, 1)

            def map_turn(i, n):
                pe.wait_ge(w_ok, i * 4 + (n + 3))
                pe.wait_ge(wt_ok, i * 4 + (n + 1))
                for c in range(4):
                    j = pe.transpose(YB[:, c * P:(c + 1) * P], wmt[:, n % 2, c * P:(c + 1) * P], ident)
                j.then_inc(wt_mm, 1)

            def by_v(i, n):
                pe.wait_ge(wt_ok, i * 4 + (n + 2))
                pe.wait_ge(os_ok, i * 4 + (n + 1))
                for c in range(4):
                    j = pe.matmul(AB[:, 0:P], wT[:, n % 2, c * P:(c + 1) * P], v[:, c, bass.ds(i * 256 + (n // 2) * P, P)],
                                  start=(c == 0), stop=(c == 3))
                j.then_inc(pv_mm, 1)

            def rotate(i):
                pe.wait_ge(qk_ok, i * 4 + 5)
                pe.wait_ge(os_ok, i * 4 + 1)
                pe.wait_ge(wt_ok, i * 4 + 1)
                pe.matmul(AB[:, :].rearrange("p (h t) -> p h t", h=2), perm, qst, start=True, stop=True).then_inc(rot_mm, 1)
                pe.matmul(YB[:, :].rearrange("p (h t) -> p h t", h=2), perm, kst[:, :, TC:T], start=True, stop=True).then_inc(rot_mm, 1)

            def q_and_k(i, u, hq=None, hk=None):
                pe.wait_ge(qk_ok, i * 4 + 1)
                gemm(u, [(j, GB[j][:, 0:TC]) for j in range(2)], H, range(KC), 0, KC - 1, t0=TC, hooks=hq)
                pe.wait_ge(qk_ok, i * 4 + 3)
                gemm(u.plus(1), [(j, GB[j][:, :]) for j in range(2)], H, range(KC), 0, KC - 1, hooks=hk)

            pe.wait_ge(v_ok, 12)
            q_and_k(0, Unit(U_QK))
            rotate(0)
            with pe.Fori(1, 4) as i:
                j = i - 1
                q_and_k(i, Unit(U_QK, 2, i),
                        {0: lambda: scores(j, 0), 2: lambda: scores(j, 1), 5: lambda: map_turn(j, 0),
                         7: lambda: (by_v(j, 0), scores(j, 2))},
                        {1: lambda: map_turn(j, 1), 2: lambda: (by_v(j, 1), scores(j, 3)), 4: lambda: map_turn(j, 2),
                         5: lambda: by_v(j, 2), 6: lambda: map_turn(j, 3), 7: lambda: by_v(j, 3)})
                rotate(i)
            scores(3, 0)
            for n in range(4):
                if n < 3:
                    scores(3, n + 1)
                map_turn(3, n)
                by_v(3, n)
            for j in range(4):
                hq, qb = j // 2, j % 2
                pe.wait_ge(on_ok, qb + 1)
                for h in range(4):
                    t = pe.transpose(OTB[j][:, h * P:(h + 1) * P], osb[:, qb, 4 * hq + h, :], ident)
                t.then_inc(ot_mm, 1)
            pe.wait_ge(o_ok, 4)
            with pe.Fori(0, 2) as i:
                for m in range(2):
                    pe.wait_ge(xup, i * 4 + (2 * m + 18))
                    gemm(Unit(U_WO + m, 2, i), [(j, GB[2 * m + j][:, TC:T]) for j in range(2)], (oh, ol), range(KC), 0, KC - 1, t0=0, t1=TC)
            norm(4, 2, SQ_X[5])
            ffn(1, U_GU1, U_DN1, TC, 3 * KC)
            norm(5, 2, SQ_X[5] + KC)


def packed(w, units):
    k = w.shape[0] // P
    return np.ascontiguousarray(w.reshape(k, P, units, UN).transpose(2, 1, 0, 3).reshape(units, P, k * UN))


def constants():
    i = np.arange(P)
    perm = (i[:, None] == (i ^ 32)[None, :]).astype(np.float32)
    pairs, width, grid = 16, TC, 64
    freqs = (1.0 / (np.float32(10000.0) ** (np.arange(pairs, dtype=np.float32) / np.float32(pairs)))).astype(np.float32)
    t = np.arange(width)
    row, colm = (t // grid).astype(np.float32), (t % grid).astype(np.float32)
    ang = np.concatenate([row[:, None] * freqs, colm[:, None] * freqs], axis=1)
    cos, sin = np.cos(ang).T[i % 32], np.sin(ang).T[i % 32]
    sin = np.where((i % 64 < 32)[:, None], -sin, sin)
    keep = np.concatenate([np.eye(P), np.ones((P, P)), perm, cos, sin], axis=1).astype(np.float32)
    fw, bw = i[:, None] <= i[None, :], i[:, None] >= i[None, :]
    stage = np.concatenate([fw, bw, np.where(fw, 0.0, NEG), np.where(bw, 0.0, NEG)], axis=1).astype(np.float32)
    return keep, stage


def kernel(**inputs):
    import concourse.bacc as bacc
    from concourse.bass_utils import run_bass_kernel_spmd

    a = {n: np.asarray(w) for n, w in inputs.items()}

    def chunks(w):
        return w.reshape(-1, P).T

    def rows(w):
        return np.broadcast_to(w.reshape(1, -1), (P, w.size))

    cw, cb = a["ssd_conv_w"][0], a["ssd_conv_b"][0]
    taps = []
    for g in range(NG):
        starts = [DI + g * P, DI + NG * P + g * P] + [g * 512 + q * P for q in range(QT)]
        for s in starts:
            taps += [cw[:, s:s + P].T, cb[s:s + P, None]]
    parts = {
        "n1w": chunks(a["norm1_w"]), "n2w": chunks(a["norm2_w"]), "fnw": chunks(a["final_norm_w"]),
        "bada": chunks(a["b_ada"]), "conv": np.concatenate(taps, axis=1),
        "dskip": chunks(np.repeat(a["ssd_d"][0], HP)), "gnw": chunks(a["ssd_norm_w"][0]), "subln": chunks(a["da_subln_w"][0]),
        "dtb": rows(a["ssd_dt_bias"][0]), "alog": rows(a["ssd_a_log"][0]),
        "lqk": rows(np.concatenate([a["da_lq1"][0], a["da_lq2"][0], a["da_lk1"][0], a["da_lk2"][0]])),
        "cvec": np.stack([chunks(a["c_ctx"]), chunks(a["c"][0])], axis=2).reshape(P, 2 * KC),
    }
    cols = np.concatenate([parts[n] for n, _ in _sizes], axis=1)
    assert cols.shape == (P, NCOL)
    keep, stage = constants()
    tok = np.concatenate([a["ctx"][0], a["x"][0]], axis=0)
    xT = tok.T.reshape(KC, P, T).transpose(1, 0, 2)

    w_in = a["ssd_w_in"][0]
    def in_cols(s, n):
        return w_in[:, s:s + n].reshape(KC, P, n).transpose(1, 0, 2).reshape(P, KC * n)

    B0, C0, DT0 = 2 * DI, 2 * DI + NG * P, 2 * DI + 2 * NG * P
    wxg = np.stack([np.concatenate([in_cols(B0 + g * P, P), in_cols(C0 + g * P, P), in_cols(DI + g * 512, UN),
                                    in_cols(DI + g * 512 + UN, UN)], axis=1) for g in range(NG)])
    wout = a["ssd_w_out"][0]
    wout = np.stack([packed(wout[h * D:(h + 1) * D], 4) for h in range(2)], axis=1).reshape(8, P, UF)
    gate, up = a["ffn_w_gate"], a["ffn_w_up"]
    wgu = np.concatenate([np.stack([packed(gate[l], FC // 2), packed(up[l], FC // 2)], axis=1).reshape(FC, P, UF) for l in range(2)])
    wdn = np.concatenate([packed(a["ffn_w_down"][l], 4) for l in range(2)])
    wq, wk, wv = [packed(a["da_w_qkv"][0][:, i * D:(i + 1) * D], 4) for i in range(3)]
    data = {
        "cols": cols, "keep": keep, "stage": stage, "xT": xT,
        "wada": packed(a["w_ada"][0], 24)[0:ADA_PE],
        "wadaT": np.concatenate([w.T.reshape(24, 2, P, D).transpose(0, 2, 1, 3) for w in a["w_ada"]])[ADA_PE:],
        "crow": rows(np.concatenate([a["c_ctx"], a["c"][0]])),
        "wdt": in_cols(DT0, 64), "wxg": wxg, "wz": packed(w_in[:, 0:DI], 8), "wout": wout, "wgu": wgu, "wdn": wdn,
        "wv": wv, "wqk": np.stack([wq, wk], axis=1).reshape(8, P, UF), "wo": packed(a["da_w_o"][0], 4),
    }
    data = {n: np.ascontiguousarray(w) for n, w in data.items()}

    nc = bacc.Bacc("TRN2", target_bir_lowering=False, num_devices=1)
    t = {n: nc.dram_tensor(n, list(w.shape), F32, kind="ExternalInput") for n, w in data.items()}
    out = nc.dram_tensor("out", [P, KC, TC], F32, kind="ExternalOutput")
    build(nc, *[t[n].ap() for n in data], out.ap())
    nc.compile()
    y = run_bass_kernel_spmd(nc, [data], core_ids=[0]).results[0]["out"]
    return np.asarray(y).reshape(P, KC, TC).transpose(2, 1, 0).reshape(1, TC, D)
```

```python
import math
from contextlib import ExitStack

import numpy as np

import concourse.bass as bass
from concourse import mybir

F32 = mybir.dt.float32
F16 = mybir.dt.float16
BF16 = mybir.dt.bfloat16
ALU = mybir.AluOpType
ACT = mybir.ActivationFunctionType
AXX = mybir.AxisListType.X

P = 128
D = 1024
KC = D // P
TC = 256
T = 2 * TC
DI = 2048
NG = 4
NH = 32
HG = NH // NG
HP = 64
QT = DI // NG // P
NCH = T // P
FF = 2816
FC = FF // P
UN = 256
UF = KC * UN
EPS = 1e-6
WS = 64.0
AS = 16.0
FS = 4.0
DS = 16.0
LAMBDA_INIT = 0.8 - 0.6 * math.exp(-0.3)
TINY = float(np.finfo(np.float32).tiny)
NEG = -1e30
AHEADS = 8

_sizes = [("n1w", 2 * KC), ("n2w", 2 * KC), ("fnw", KC), ("bada", 96), ("conv", NG * 36), ("dskip", 16),
          ("gnw", 16), ("subln", 1), ("dtb", 64), ("alog", 64), ("lqk", 256), ("cvec", 2 * KC)]
COL, _at = {}, 0
for _n, _s in _sizes:
    COL[_n] = (_at, _at + _s)
    _at += _s
NCOL = _at
K_ID, K_ONE, K_PERM, K_COS, K_SIN, NKEEP = 0, 128, 256, 384, 640, 896
S_TF, S_TB, S_NF, S_NB, NSTAGE = 0, 128, 256, 384, 512

U_SSD0 = 0
U_GRP = 4
U_TAIL = U_GRP + 6 * (NG - 1)
U_OUT = U_TAIL + 2
U_GU0 = U_OUT + 8
U_DN0 = U_GU0 + FC
U_V = U_DN0 + 12
U_QK = U_V + 4
U_WO = U_QK + 8
U_GU1 = U_WO + 4
U_DN1 = U_GU1 + FC
DNK = [(0, 8), (8, 15), (15, 22)]
ADA_FIRST = 8
ADA_HALF = ADA_FIRST // 2
ADA_PE = ADA_FIRST + NG
ADA_OUT = 8
ADA_GU = FC


class Unit:

    def __init__(self, base, per=0, i=None):
        self.base, self.per, self.i = base, per, i
        self.slot = base % 2

    def plus(self, k):
        return Unit(self.base + k, self.per, self.i)

    @property
    def n(self):
        return self.base if self.i is None else self.i * self.per + self.base

    @property
    def half(self):
        return self.base * 2 if self.i is None else self.i * (self.per * 2) + self.base * 2

    @property
    def turn(self):
        return self.base // 2 if self.i is None else self.i * (self.per // 2) + self.base // 2


def build(nc, cols, keep, stage, xT, wada, wadaT, crow, wdt, wxg, wz, wout, wgu, wdn, wv, wqk, wo, out):
    ctx = ExitStack()
    with ctx:
        def sb(name, shape, dt=F32):
            return ctx.enter_context(nc.sbuf_tensor(name, shape, dt))

        def sem(name):
            return ctx.enter_context(nc.semaphore(name))

        x = sb("x", [P, KC, T])
        hh = sb("hh", [P, KC, T], F16)
        hl = sb("hl", [P, KC, T], F16)
        raw = sb("raw", [P, 2, UF])
        wh = sb("wh", [P, 2, UF], F16)
        wl = sb("wl", [P, 2, UF], F16)
        araw = sb("araw", [P, UF])
        col = sb("col", [P, NCOL])
        kp = sb("kp", [P, NKEEP])
        masks = sb("masks", [P, 3, P], F16)
        negm = sb("negm", [P, 2, P], BF16)
        idb = sb("idb", [P, P], BF16)
        s2 = sb("s2", [P, KC, 2])
        adac = sb("adac", [P, 2, 48, 2])
        wsc = sb("wsc", [P, KC, 2])
        wsh = sb("wsh", [P, KC, 2])
        gcol = sb("gcol", [P, KC, 2])
        small = sb("small", [P, 64])
        sq = sb("sq", [P, 2, T])
        ssq = sb("ssq", [P, T])
        AR = 30640
        arena = sb("arena", [P, AR])
        at = [0]

        def carve(n):
            a = at[0]
            at[0] += n
            assert at[0] <= AR, at[0]
            return arena[:, a:a + n]

        nt = carve(2 * T).rearrange("p (b t) -> p b t", b=2)
        n32 = carve(2 * T).rearrange("p (b t) -> p b t", b=2)
        rdg = carve(T)
        mark = at[0]
        afirst = carve(ADA_HALF * UF).rearrange("p (u f) -> p u f", u=ADA_HALF)
        aturned = carve(ADA_HALF * UF).rearrange("p (u m k) -> p u m k", u=ADA_HALF, m=2)
        afdump = carve(4 * D // 2).bitcast(BF16).rearrange("p (a k) -> p a k", a=4)
        stg = carve(NSTAGE)
        at[0] = mark
        ya, yb = nt[:, 0, :], nt[:, 1, :]
        gt = n32
        G = carve(16 * T).rearrange("p (q t) -> p q t", q=16)
        pre = carve(2 * 520).rearrange("p (b s t) -> p b s t", b=2, s=2)
        acc = rdg
        xbc = carve(6 * T).rearrange("p (q t) -> p q t", q=6)
        xD = carve(QT * T).rearrange("p (q t) -> p q t", q=QT)
        Cc, Bt, cb = carve(T), carve(T), carve(T).rearrange("p (c l) -> p c l", c=NCH)
        xt = carve(NCH * 512).rearrange("p (c f) -> p c f", c=NCH)
        xdd = carve(2 * 512).rearrange("p (b f) -> p b f", b=2)
        Hs = carve(6 * 512).rearrange("p (k f) -> p k f", k=6)
        E = carve(4 * 512).rearrange("p (b d h l) -> p b d h l", b=2, d=2, h=4)
        ys = carve(2 * 512).rearrange("p (b f) -> p b f", b=2)
        PR = carve(5 * 256).rearrange("p (q c h) -> p q c h", q=5, c=8)
        PRg = carve(5 * 64).rearrange("p (q c h) -> p q c h", q=5, c=8)
        dg = carve(4)
        adh = carve(128).bitcast(F16)
        adl = carve(128).bitcast(F16)
        adgh = carve(32).bitcast(F16)
        adgl = carve(32).bitcast(F16)
        LDT, DST, DOUT, NEGA, DCH = range(5)
        dtraw = E[:, 0, 0].rearrange("p h l -> p (h l)")
        dth = E[:, 0, 1, 0:2].rearrange("p h l -> p (h l)").bitcast(F16)
        dtl = E[:, 0, 1, 2:4].rearrange("p h l -> p (h l)").bitcast(F16)
        dx, de = ys[:, 0, 0:256], ys[:, 0, 256:512]
        dz, dz2 = ys[:, 1, 0:256], ys[:, 1, 256:512]
        dq, dr = xdd[:, 0, 0:256], xdd[:, 0, 256:512]
        da = xdd[:, 1, 0:64]
        gb = mark + 16 * T
        gh = arena[:, gb:gb + 4096].bitcast(F16).rearrange("p (q t) -> p q t", q=16)
        gl = arena[:, gb + 4096:gb + 8192].bitcast(F16).rearrange("p (q t) -> p q t", q=16)
        at[0] = gb + 8192
        abuf = carve(2 * UF).rearrange("p (b m k) -> p b m k", b=2, m=2)
        adump = carve(4 * D // 2).bitcast(BF16).rearrange("p (a k) -> p a k", a=4)
        at[0] = mark
        ah = carve(FC * T // 2).bitcast(F16).rearrange("p (q t) -> p q t", q=FC)
        al = carve(FC * T // 2).bitcast(F16).rearrange("p (q t) -> p q t", q=FC)
        sg = carve(2 * T).rearrange("p (b t) -> p b t", b=2)
        a32 = carve(2 * T).rearrange("p (b t) -> p b t", b=2)
        at[0] = mark
        v = carve(4 * D).rearrange("p (c f) -> p c f", c=4)
        qst, qr = carve(512).rearrange("p (h t) -> p h t", h=2), carve(512).rearrange("p (h t) -> p h t", h=2)
        kst, kr = carve(1024).rearrange("p (h t) -> p h t", h=2), carve(1024).rearrange("p (h t) -> p h t", h=2)
        r1, r2 = carve(512).rearrange("p (h t) -> p h t", h=2), carve(512).rearrange("p (h t) -> p h t", h=2)
        EA = carve(4 * 512).rearrange("p (b m k) -> p b m k", b=2, m=2)
        wmt = carve(2 * 512).rearrange("p (b k) -> p b k", b=2)
        wT = carve(2 * 512).rearrange("p (b k) -> p b k", b=2)
        osb = carve(2 * D).rearrange("p (b h e) -> p b h e", b=2, h=AHEADS)
        osq = carve(128)
        o32 = carve(2 * 512).rearrange("p (b f) -> p b f", b=2)
        oh = carve(1024).bitcast(F16).rearrange("p (h t) -> p h t", h=AHEADS)
        ol = carve(1024).bitcast(F16).rearrange("p (h t) -> p h t", h=AHEADS)
        mx = carve(4).rearrange("p (b m) -> p b m", b=2)
        nb = carve(4).rearrange("p (b m) -> p b m", b=2)
        es = carve(4).rearrange("p (b m) -> p b m", b=2)
        rs = carve(4).rearrange("p (b m) -> p b m", b=2)
        oss = carve(16).rearrange("p (b h) -> p b h", b=2)
        ort = carve(16).rearrange("p (b h) -> p b h", b=2)
        lp = carve(128).rearrange("p (a d) -> p a d", a=2)
        ls = carve(2)
        nlam = carve(1)
        fin = arena[:, mark:mark + KC * TC].rearrange("p (k t) -> p k t", k=KC)

        ident, ones, perm = kp[:, K_ID:K_ID + P], kp[:, K_ONE:K_ONE + P], kp[:, K_PERM:K_PERM + P]
        cosT, sinT = kp[:, K_COS:K_COS + TC], kp[:, K_SIN:K_SIN + TC]
        eps = small[:, 0:1]
        rt = small[:, 4:8]

        def cc(name, a=0, b=None):
            lo, hi = COL[name]
            return col[:, lo + a:(hi if b is None else lo + b)]

        bank = [ctx.enter_context(nc.psum_tensor(f"bank{i}", [P, 512], F32)) for i in range(8)]
        GB = bank[0:4]
        DB = bank[2:4]
        YB, OB, AB = bank[4], bank[5:7], bank[7]
        SB = [(bank[2], bank[3]), (bank[5], bank[6])]
        OTB = [bank[2], bank[3], bank[5], bank[6]]

        in_col, in_kp, in_stage, in_x, in_dt = [sem(n) for n in ("in_col", "in_kp", "in_stage", "in_x", "in_dt")]
        in_ada = [sem(f"in_ada{i}") for i in range(ADA_HALF)]
        in_turned = [sem(f"in_turned{i}") for i in range(ADA_HALF)]
        ada0_sum = sem("ada0_sum")
        raw_in = [sem("raw_in0"), sem("raw_in1")]
        araw_in, out_done = sem("araw_in"), sem("out_done")
        crow_in, srow_ok = sem("crow_in"), sem("srow_ok")
        abuf_in = [sem("abuf_in0"), sem("abuf_in1")]
        ada_sum, ada_ok = sem("ada_sum"), sem("ada_ok")
        hi_done, lo_done = sem("hi_done"), sem("lo_done")
        unit_done = sem("unit_done")
        LO = UD = 4
        masks_ok, s2_ok, eps_ok = sem("masks_ok"), sem("s2_ok"), sem("eps_ok")
        a0_mm = sem("a0_mm")
        cols_ok = sem("cols_ok")
        sqd, ssd = sem("sqd"), sem("ssd")
        c_ss, c_rt, c_rr, c_dg, c_bc = [sem(n) for n in ("c_ss", "c_rt", "c_rr", "c_dg", "c_bc")]
        nt_ok, n32_ok, hh_ok, h_ok = sem("nt_ok"), sem("n32_ok"), sem("hh_ok"), sem("h_ok")
        xup = sem("xup")
        dth_ok, dtl_ok, dt_mm, dta, dtv, adt_ok = [sem(n) for n in ("dth_ok", "dtl_ok", "dt_mm", "dta", "dtv", "adt_ok")]
        A_mm, aexp, pr_ok, pads_ok = sem("A_mm"), sem("aexp"), sem("pr_ok"), sem("pads_ok")
        pre_ok, conv, conv_ok, xbc_ok, zs_ok = [sem(n) for n in ("pre_ok", "conv", "conv_ok", "xbc_ok", "zs_ok")]
        o_mm = [sem("o_mm0"), sem("o_mm1")]
        o_free = [sem("o_free0"), sem("o_free1")]
        prg_ok, xD_ok, xdd_ok, hm_ok, bt_ok = [sem(n) for n in ("prg_ok", "xD_ok", "xdd_ok", "hm_ok", "bt_ok")]
        d_mm, e_ok, t_ok, yd = sem("d_mm"), sem("e_ok"), sem("t_ok"), sem("yd")
        yp, y_ok = sem("yp"), sem("y_ok")
        a_mm, a_free = sem("a_mm"), sem("a_free")
        g_ok = sem("g_ok")
        gn_t, gn_h, gn_ok = sem("gn_t"), sem("gn_h"), sem("gn_ok")
        sg_ok, a32_ok, ah_ok, al_ok = sem("sg_ok"), sem("a32_ok"), sem("ah_ok"), sem("al_ok")
        v_ok, qk_ok, rot_mm, rope, qkr_ok, lam = [sem(n) for n in ("v_ok", "qk_ok", "rot_mm", "rope", "qkr_ok", "lam")]
        s_mm, mx_ok, nb_ok, ea_ok, rs_ok, w_t, w_ok = [sem(n) for n in ("s_mm", "mx_ok", "nb_ok", "ea_ok", "rs_ok", "w_t", "w_ok")]
        wt_mm, wt_ok, pv_mm, os_ok = sem("wt_mm"), sem("wt_ok"), sem("pv_mm"), sem("os_ok")
        ort_s, ort_ok, on_ok, ot_mm, o32_ok, oh_ok, o_ok = [sem(n) for n in ("ort_s", "ort_ok", "on_ok", "ot_mm", "o32_ok", "oh_ok", "o_ok")]
        fin_ok = sem("fin_ok")
        ln_ok, tsum = sem("ln_ok"), sem("tsum")
        apart = sem("apart")

        O_PER = 9
        O_B, O_CB = (0, 0), (1, 0)
        O_XT = [(0, 1), (1, 1), (0, 2), (1, 2)]
        O_ST = [(0, 3), (1, 3), (0, 4), (1, 4), (0, 5), (1, 5)]
        ST = [(0, 0), (1, 1), (1, 0), (0, 1), (2, 0), (3, 1)]
        ST_FROM = [None, None, 0, 1, 2, 3]
        YOFF = [{1: (1, 6)}, {0: (0, 6)}, {0: (2, 7), 1: (5, 7)}, {0: (4, 8), 1: (3, 8)}]
        A_PER = 5
        A_ADA = 3
        A_YT = [0, 1, 2, 4]
        SQ_G = KC
        SQ_X = [0, None, SQ_G + 16, SQ_G + 16 + KC, SQ_G + 16 + 2 * KC, SQ_G + 16 + 3 * KC]
        HN = {0: 0, 2: 1, 3: 2, 4: 3}

        block = ctx.enter_context(nc.Block())

        @block.sync
        def _(sp):
            sp.dma_start(col[:, :], cols).then_inc(in_col, 16)
            def load_first(n):
                sp.dma_start(afirst[:, n, :], wada[n]).then_inc(in_ada[n], 16)

            def load_turned(n):
                sp.dma_start(aturned[:, n], wadaT[n]).then_inc(in_turned[n], 16)

            load_first(0)
            sp.dma_start(araw[:, :], crow).then_inc(crow_in, 16)
            load_turned(0)
            load_first(1)
            load_first(2)
            load_turned(1)
            sp.dma_start(x[:, :, :], xT).then_inc(in_x, 16)
            sp.dma_start(kp[:, :], keep).then_inc(in_kp, 16)
            load_first(3)
            load_turned(2)
            load_turned(3)
            sp.dma_start(stg, stage).then_inc(in_stage, 16)
            sp.dma_start(dtraw, wdt).then_inc(in_dt, 16)

            def load(u, src, n=UF):
                sp.wait_ge(lo_done, u.half + 2)
                sp.dma_start(raw[:, u.slot, 0:n], src).then_inc(raw_in[u.slot], 16)

            def load_group(u, g):
                for k, (a, b) in enumerate([(0, 1024), (1024, 2048), (2048, 4096), (4096, 6144)]):
                    load(u.plus(k), wxg[g, :, a:b], b - a)

            load_group(Unit(U_SSD0), 0)
            with sp.Fori(0, NG - 1) as g:
                u = Unit(U_GRP, 6, g)
                load(u, wz[g * 2])
                load(u.plus(1), wz[g * 2 + 1])
                load_group(u.plus(2), g + 1)
            for k in range(2):
                load(Unit(U_TAIL + k), wz[2 * (NG - 1) + k])

            def pairs(n, first, src, at=0):
                with sp.Fori(0, n) as i:
                    for k in range(2):
                        load(Unit(first + k, 2, i), src[i * 2 + (at + k)])

            def ffn(layer, ugu, udn):
                pairs(FC // 2, ugu, wgu, layer * FC)
                for m in range(4):
                    for k, (a, b) in enumerate(DNK):
                        load(Unit(udn + 3 * m + k), wdn[layer * 4 + m, :, a * UN:b * UN], (b - a) * UN)

            pairs(4, U_OUT, wout)
            ffn(0, U_GU0, U_DN0)
            pairs(2, U_V, wv)
            pairs(4, U_QK, wqk)
            pairs(2, U_WO, wo)
            ffn(1, U_GU1, U_DN1)
            for b in range(2):
                sp.wait_ge(fin_ok, 4 * b + 4)
                sp.dma_start(out[:, 4 * b:4 * b + 4, :], fin[:, 4 * b:4 * b + 4, :]).then_inc(out_done, 16)
            sp.wait_ge(out_done, 32)

        @block.scalar
        def _(act):
            def alone():
                act.sem_inc(apart, 1)

            def cvt_half(u, j, a, b, whole=0):
                if j == 0:
                    act.wait_ge(raw_in[u.slot], u.turn * 16 + 16)
                act.wait_ge(unit_done, u.half + (UD - 3 + j + whole))
                act.activation(wh[:, u.slot, a:b], raw[:, u.slot, a:b], ACT.Copy, scale=WS).then_inc(hi_done, 1)

            def cvt(u, n=UF):
                cvt_half(u, 0, 0, n // 2, 1)
                cvt_half(u, 1, n // 2, n)

            def cvt_on(u, n=UF):
                cvt_half(u, 1, UF // 2, n)
                if u.base < U_DN1 + 11:
                    cvt_half(u.plus(1), 0, 0, UF // 2)

            def ada_load(a, last):
                act.wait_ge(a_mm, last + 3)
                act.dma_start(araw[:, :], wada[a]).then_inc(araw_in, 16)

            def root(n, width, cs):
                act.wait_ge(c_ss, n + 1)
                act.activation(rt[:, cs:4], OB[0][:, cs:4], ACT.Sqrt, scale=1.0 / width, bias=eps).then_inc(c_rt, 1)

            def square_pair(n, k, t0, up):
                for m in range(2):
                    act.wait_ge(xup, up + (m + 5))
                    act.wait_ge(ssd, n + (m - 1))
                    alone()
                    act.activation(sq[:, m, None, t0:T], x[:, bass.ds(k + m, 1), t0:T], ACT.Square).then_inc(sqd, 1)

            def h_hi(n, t0):
                for k in range(KC):
                    act.wait_ge(n32_ok, HN[n] * KC + k + 1)
                    act.activation(hh[:, k, t0:T], n32[:, k % 2, t0:T], ACT.Copy).then_inc(hh_ok, 1)

            def evac_pre(u, g, tile, b):
                act.wait_ge(unit_done, u.half + (UD + 2))
                act.wait_ge(conv_ok, g * 6 + (tile + 1))
                act.activation(pre[:, tile % 2, :, 2:258], GB[b][:, :].rearrange("p (s t) -> p s t", s=2), ACT.Copy,
                               scale=1.0 / (WS * AS)).then_inc(pre_ok, 1)

            def silu_xbc(g, tile):
                act.wait_ge(conv_ok, g * 6 + (tile + 3))
                if tile == 0 and not isinstance(g, int):
                    act.wait_ge(xD_ok, g * QT)
                act.activation(xbc[:, tile, :], acc, ACT.Silu).then_inc(xbc_ok, 1)

            def exps(g, c, between=None):
                for q in range(4):
                    n = g * 16 + (4 * c + q)
                    d, hq = q % 2, q // 2
                    act.wait_ge(d_mm, n + 1)
                    act.wait_ge(yd, g * 8 + (2 * c + hq + 1))
                    for h in range(4):
                        i = act.activation(E[:, hq, d, h, :], DB[q % 2][:, h * P:(h + 1) * P], ACT.Exp, scale=1.0 / DS,
                                           bias=PRg[:, NEGA, 2 * c + d, 4 * hq + h:4 * hq + h + 1])
                    i.then_inc(e_ok, 1)
                    if between and q in between:
                        between[q]()

            def z_out(u, g, k):
                act.wait_ge(unit_done, u.half + (UD + 2))
                alone()
                for m in range(2):
                    act.activation(G[:, bass.ds(g * QT + (2 * k + m), 1), :], GB[2 - 2 * k + m][:, None, :], ACT.Silu,
                                   scale=1.0 / (WS * AS)).then_inc(zs_ok, 1)

            def group(g, u, more):
                cvt(u.plus(1))
                ada_load(g + ADA_HALF, g * A_PER - 1)
                act.wait_ge(o_mm[0], g * O_PER + (O_B[1] + 1))
                act.activation(Bt, OB[0][:, :], ACT.Copy).then_inc(o_free[0], 1)
                act.wait_ge(o_mm[1], g * O_PER + (O_CB[1] + 1))
                act.activation(cb.rearrange("p c l -> p (c l)"), OB[1][:, :], ACT.Copy).then_inc(o_free[1], 1)
                act.activation(Cc, xbc[:, 1, :], ACT.Copy).then_inc(bt_ok, 1)
                z_out(u, g, 0)
                cvt(u.plus(2), 1024 if more else UF)
                for k in range(2):
                    act.wait_ge(o_mm[k], g * O_PER + (O_ST[k][1] + 1))
                    act.activation(Hs[:, k, :], OB[k][:, :], ACT.Copy).then_inc(o_free[k], 1)
                z_out(u.plus(1), g, 1)
                if more:
                    cvt(u.plus(3), 1024)
                exps(g, 0)
                if more:
                    evac_pre(u.plus(2), g + 1, 0, 0)
                    cvt(u.plus(4))
                exps(g, 1)
                if more:
                    evac_pre(u.plus(3), g + 1, 1, 1)
                    silu_xbc(g + 1, 0)
                    cvt(u.plus(5))
                exps(g, 2)
                if more:
                    evac_pre(u.plus(4), g + 1, 2, 0)
                    evac_pre(u.plus(4), g + 1, 3, 1)
                    silu_xbc(g + 1, 1)
                    cvt(u.plus(6))
                exps(g, 3, {1: lambda: silu_xbc(g + 1, 2)} if more else None)
                if more:
                    evac_pre(u.plus(5), g + 1, 4, 0)
                    silu_xbc(g + 1, 3)
                    evac_pre(u.plus(5), g + 1, 5, 1)
                else:
                    act.wait_ge(a_mm, g * A_PER + (A_ADA + 3))
                    act.dma_start(araw[:, :], crow).then_inc(crow_in, 16)
                act.wait_ge(g_ok, g * NCH + (NCH + 2))
                for q in range(QT):
                    act.wait_ge(ssd, g * QT + (SQ_G + q - 1))
                    alone()
                    act.activation(sq[:, q % 2, None, :], G[:, bass.ds(g * QT + q, 1), :], ACT.Square).then_inc(sqd, 1)
                if more:
                    silu_xbc(g + 1, 4)
                    silu_xbc(g + 1, 5)

            for s, n in [(e_ok, 2), (sg_ok, 2), (v_ok, 4), (qk_ok, 1), (ea_ok, 2), (wt_ok, 1), (os_ok, 1)]:
                act.sem_inc(s, n)
            act.wait_ge(in_col, 16)
            act.activation(s2[:, :, :], cc("cvec").rearrange("p (k b) -> p k b", b=2), ACT.Silu).then_inc(s2_ok, 1)
            act.wait_ge(crow_in, 16)
            act.activation(araw[:, :], araw[:, :], ACT.Silu).then_inc(srow_ok, 1)
            act.wait_ge(in_x, 16)
            for k in range(KC):
                if k >= 2:
                    act.wait_ge(ssd, k - 1)
                act.activation(sq[:, k % 2, :], x[:, k, :], ACT.Square).then_inc(sqd, 1)
            act.wait_ge(eps_ok, 1)
            root(0, D, 0)
            act.wait_ge(in_stage, 16)
            act.activation(masks[:, 0:2, :], stg[:, S_TF:S_TF + 256].rearrange("p (a l) -> p a l", a=2), ACT.Copy).then_inc(masks_ok, 1)
            act.activation(negm[:, :, :], stg[:, S_NF:S_NF + 256].rearrange("p (a l) -> p a l", a=2), ACT.Copy).then_inc(masks_ok, 1)
            act.wait_ge(in_kp, 16)
            act.activation(masks[:, 2, :], ones, ACT.Copy).then_inc(masks_ok, 1)
            act.activation(idb[:, :], ident, ACT.Copy).then_inc(masks_ok, 1)
            act.wait_ge(in_dt, 16)
            act.activation(dth, dtraw, ACT.Copy, scale=WS).then_inc(dth_ok, 1)
            cvt(Unit(U_SSD0), 1024)
            h_hi(0, 0)
            cvt(Unit(U_SSD0 + 1), 1024)
            cvt(Unit(U_SSD0 + 2))

            act.wait_ge(pads_ok, 2)
            evac_pre(Unit(U_SSD0), 0, 0, 0)
            act.wait_ge(dtv, 1)
            act.activation(de, dx, ACT.Abs).then_inc(dta, 1)
            act.wait_ge(dta, 1)
            act.activation(de, de, ACT.Exp, scale=-1.0).then_inc(dta, 1)
            act.activation(da, cc("alog"), ACT.Exp).then_inc(dta, 1)

            u = Unit(U_SSD0)
            silu_xbc(0, 0)
            evac_pre(u.plus(1), 0, 1, 1)
            cvt(u.plus(3))
            ldt = PR[:, LDT].rearrange("p c h -> p (c h)")
            act.wait_ge(adt_ok, 1)
            act.activation(ldt, ldt, ACT.Ln).then_inc(ln_ok, 1)
            cvt(u.plus(4))
            silu_xbc(0, 1)
            evac_pre(u.plus(2), 0, 2, 2)
            evac_pre(u.plus(2), 0, 3, 3)
            silu_xbc(0, 2)
            silu_xbc(0, 3)
            act.wait_ge(A_mm, 1)
            act.activation(PR[:, DOUT].rearrange("p c h -> p (c h)"), OB[1][:, 0:256], ACT.Exp, scale=1.0 / DS).then_inc(aexp, 1)
            act.activation(PR[:, DCH].rearrange("p c h -> p (c h)"), OB[1][:, 256:512], ACT.Exp, scale=1.0 / DS).then_inc(aexp, 1)
            act.wait_ge(pr_ok, 2)
            dst = PR[:, DST].rearrange("p c h -> p (c h)")
            act.activation(dst, dst, ACT.Exp).then_inc(aexp, 1)
            for m in range(2):
                evac_pre(u.plus(3), 0, 4 + m, m)
                silu_xbc(0, 4 + m)
            with act.Fori(0, NG - 1) as g:
                group(g, Unit(U_GRP, 6, g), True)
            group(NG - 1, Unit(U_TAIL), False)

            cvt_half(Unit(U_OUT + 1), 0, 0, UF // 2)
            cvt_half(Unit(U_OUT + 1), 1, UF // 2, UF)
            root(1, DI, 0)
            for k in range(16):
                act.wait_ge(gn_t, k + 1)
                act.activation(gh[:, k, :], nt[:, k % 2, :], ACT.Copy).then_inc(gn_h, 1)
            act.wait_ge(crow_in, 32)
            act.activation(araw[:, :], araw[:, :], ACT.Silu).then_inc(srow_ok, 1)
            with act.Fori(0, 2) as i:
                for m in range(2):
                    u = Unit(U_OUT + 2 * m, 4, i)
                    for k in range(2, 4):
                        cvt_half(u.plus(k), 0, 0, UF // 2)
                        cvt_half(u.plus(k), 1, UF // 2, UF)
                    square_pair(i * 4 + (SQ_X[2] + 2 * m), i * 4 + 2 * m, 0, i * 4 + 2 * m)

            def ffn(layer, ugu, udn, t0, with_ada):
                n0 = layer * FC
                cvt_half(Unit(ugu + 2), 0, 0, UF // 2)
                with act.Fori(0, FC // 2) as i:
                    u = Unit(ugu, 2, i)
                    act.wait_ge(unit_done, u.half + (UD + 2))
                    for m in range(2):
                        act.wait_ge(a32_ok, i * 2 + (n0 + m + 1))
                        act.activation(sg[:, m, t0:T], GB[m][:, t0:T], ACT.Silu, scale=1.0 / (WS * AS)).then_inc(sg_ok, 1)
                    cvt_on(u.plus(2))
                    cvt_half(u.plus(3), 1, UF // 2, UF)
                    for m in range(2):
                        act.wait_ge(a32_ok, i * 2 + (n0 + m + 3))
                        alone()
                        act.activation(ah[:, bass.ds(i * 2 + m, 1), t0:T], a32[:, m, None, t0:T], ACT.Copy).then_inc(ah_ok, 1)
                    cvt_half(u.plus(4), 0, 0, UF // 2)
                for m in range(4):
                    for k in range(3):
                        nxt = Unit(udn + 3 * m + k + 1)
                        if 0 < 3 * m + k and nxt.base < U_DN1 + 12:
                            kk = (3 * m + k + 1) % 12 % 3
                            a, b = DNK[kk]
                            cvt_on(nxt, UF if 3 * m + k + 1 == 12 else (b - a) * UN)
                    square_pair(SQ_X[3 + 2 * layer] + 2 * m, 2 * m, t0, 8 + 16 * layer + 2 * m)

            root(2, D, 0)
            h_hi(2, 0)
            ffn(0, U_GU0, U_DN0, 0, True)

            root(3, D, 0)
            h_hi(3, 0)
            act.wait_ge(lam, 2)
            act.activation(ls, ls, ACT.Exp).then_inc(lam, 1)
            with act.Fori(0, 2) as i:
                cvt_on(Unit(U_V + 1, 2, i))
                cvt_on(Unit(U_V + 2, 2, i))
                act.wait_ge(unit_done, i * 4 + (2 * U_V + UD + 4))
                alone()
                for c in range(4):
                    act.activation(v[:, c, bass.ds(i * 512, 512)], GB[c][:, :], ACT.Copy, scale=1.0 / (WS * AS)).then_inc(v_ok, 1)

            def q_out(u, i):
                act.wait_ge(unit_done, u.half + (UD + 2))
                act.wait_ge(qkr_ok, i + 1)
                for m in range(2):
                    act.activation(qst[:, m, :], GB[m][:, 0:TC], ACT.Copy, scale=1.0 / (WS * AS)).then_inc(qk_ok, 1)

            def k_out(u, i):
                act.wait_ge(unit_done, u.half + (UD + 2))
                for m in range(2):
                    act.activation(kst[:, m, :], GB[m][:, :], ACT.Copy, scale=1.0 / (WS * AS)).then_inc(qk_ok, 1)

            def exp_maps(i, n):
                N = i * 4 + n
                act.wait_ge(nb_ok, N + 1)
                act.wait_ge(w_ok, N + 1)
                for m in range(2):
                    s = act.activation(EA[:, n % 2, m, :], SB[n % 2][m][:, :], ACT.Exp, scale=0.125, bias=nb[:, n % 2, m:m + 1],
                                       accum_out=es[:, n % 2, m:m + 1])
                s.then_inc(ea_ok, 1)

            def wt_out(i, n):
                act.wait_ge(wt_mm, i * 4 + (n + 3))
                act.activation(wT[:, n % 2, :], YB[:, :], ACT.Copy).then_inc(wt_ok, 1)

            def o_out(i, n):
                head, qb = i * 2 + n // 2, n % 2
                act.wait_ge(pv_mm, i * 4 + (n + 1))
                act.wait_ge(os_ok, i * 4 + (n + 1))
                alone()
                act.activation(osb[:, qb, bass.ds(head, 1), :], AB[:, None, 0:P], ACT.Copy)
                act.activation(osq, AB[:, 0:P], ACT.Square, accum_out=oss[:, qb, bass.ds(head, 1)]).then_inc(os_ok, 1)

            cvt_on(Unit(U_QK + 1))
            q_out(Unit(U_QK), 0)
            cvt_on(Unit(U_QK + 2))
            k_out(Unit(U_QK + 1), 0)
            with act.Fori(1, 4) as i:
                u = Unit(U_QK, 2, i)
                j = i - 1
                cvt_half(u.plus(1), 1, UF // 2, UF)
                cvt_half(u.plus(2), 0, 0, UF // 2)
                q_out(u, i)
                exp_maps(j, 0)
                exp_maps(j, 1)
                cvt_half(u.plus(2), 1, UF // 2, UF)
                wt_out(j, 0)
                exp_maps(j, 2)
                o_out(j, 0)
                wt_out(j, 1)
                exp_maps(j, 3)
                o_out(j, 1)
                cvt_half(u.plus(3), 0, 0, UF // 2)
                wt_out(j, 2)
                o_out(j, 2)
                wt_out(j, 3)
                k_out(u.plus(1), i)
                o_out(j, 3)
            exp_maps(3, 0)
            exp_maps(3, 1)
            for n in range(4):
                wt_out(3, n)
                if n < 2:
                    exp_maps(3, n + 2)
                o_out(3, n)
            act.wait_ge(os_ok, 17)
            act.activation(ort.rearrange("p b h -> p (b h)"), oss.rearrange("p b h -> p (b h)"), ACT.Sqrt, scale=1.0 / P, bias=eps).then_inc(ort_s, 1)
            for j in range(4):
                hq, qb = j // 2, j % 2
                act.wait_ge(o32_ok, j + 1)
                act.activation(oh[:, 4 * hq:4 * hq + 4, qb * P:(qb + 1) * P], o32[:, j % 2, :].rearrange("p (h t) -> p h t", h=4), ACT.Copy).then_inc(oh_ok, 1)
            with act.Fori(0, 2) as i:
                for m in range(2):
                    cvt_on(Unit(U_WO + m + 1, 2, i))
                    square_pair(i * 4 + (SQ_X[4] + 2 * m), i * 4 + 2 * m, TC, i * 4 + (16 + 2 * m))
            cvt_half(Unit(U_GU1 + 1), 1, UF // 2, UF)
            root(4, D, 2)
            h_hi(4, TC)
            ffn(1, U_GU1, U_DN1, TC, False)
            root(5, D, 2)

        @block.vector
        def _(ve):
            steps = [0]

            def step(i):
                i.then_inc(cols_ok, 1)
                steps[0] += 1
                ve.wait_ge(cols_ok, steps[0])

            def cvt_half(u, j, a, b):
                ve.wait_ge(hi_done, u.half + (j + 1))
                ve.scalar_tensor_tensor(wl[:, u.slot, a:b], raw[:, u.slot, a:b], WS, wh[:, u.slot, a:b], ALU.mult,
                                        ALU.subtract).then_inc(lo_done, 1)

            def cvt(u, n=UF):
                cvt_half(u, 0, 0, n // 2)
                cvt_half(u, 1, n // 2, n)

            def cvt_on(u, n=UF):
                cvt_half(u, 1, UF // 2, n)
                if u.base < U_DN1 + 11:
                    cvt_half(u.plus(1), 0, 0, UF // 2)

            asum = small[:, 40:44].rearrange("p (m c) -> p m c", m=2)
            adaf = adac[:, :, :, :].rearrange("p l c b -> p (l c) b")

            def ada_out(a, fill):
                ve.wait_ge(a_mm, fill + 3)
                bias = cc("bada")[:, bass.ds(a * 2, 2)]
                ve.tensor_tensor(adaf[:, bass.ds(a * 2, 2), :], AB[:, 0:4].rearrange("p (c b) -> p c b", b=2),
                                 bias[:, :, None].to_broadcast([P, 2, 2]), ALU.add).then_inc(a_free, 1)

            def ada_unit(k, b):
                ve.wait_ge(srow_ok, 2)
                ve.wait_ge(abuf_in[b], k * 8 + (16 - 8 * b))
                ve.wait_ge(ada_ok, k)
                for m in range(2):
                    for c in range(2):
                        i = ve.scalar_tensor_tensor(adump[:, 2 * m + c, :], abuf[:, b, m, :], 1.0, araw[:, c * D:(c + 1) * D], ALU.mult, ALU.mult,
                                                    accum_out=asum[:, m, c:c + 1])
                i.then_inc(ada_sum, 1)
                ve.wait_ge(ada_sum, k + 1)
                at_ = bass.ds(k * 2 + 2 * ADA_PE, 2)
                ve.tensor_tensor(adaf[:, at_, :], asum, cc("bada")[:, at_][:, :, None].to_broadcast([P, 2, 2]), ALU.add).then_inc(ada_ok, 1)

            def columns(l, norm_w, shift):
                step(ve.scalar_tensor_tensor(wsc[:, :, :], adac[:, l, shift + KC:shift + 2 * KC, :], 1.0,
                                             norm_w[:, :, None].to_broadcast([P, KC, 2]), ALU.add, ALU.mult))
                step(ve.tensor_scalar(wsc[:, :, :], wsc[:, :, :], AS, None, ALU.mult))
                step(ve.tensor_scalar(wsh[:, :, :], adac[:, l, shift:shift + KC, :], AS, None, ALU.mult))

            def gates(l, at, scale):
                step(ve.tensor_scalar(gcol[:, :, :], adac[:, l, at:at + KC, :], 1.0 / scale, None, ALU.mult))

            def inverse(n, cs):
                ve.wait_ge(c_rt, n + 1)
                ve.reciprocal(rt[:, cs:4], rt[:, cs:4]).then_inc(c_rr, 1)
                ve.wait_ge(c_rr, n + 1)
                ve.tensor_tensor(rdg[:, cs * P:T].rearrange("p (c l) -> p c l", l=P),
                                 ident[:, None, :].to_broadcast([P, 4 - cs, P]),
                                 rt[:, cs:4][:, :, None].to_broadcast([P, 4 - cs, P]), ALU.mult).then_inc(c_dg, 1)

            def add_square(n, t0, b):
                ve.wait_ge(sqd, n + 1)
                ve.wait_ge(ssd, n)
                ve.tensor_tensor(ssq[:, t0:T], ssq[:, t0:T], sq[:, b, t0:T], ALU.add).then_inc(ssd, 1)

            def h_lo(n, t0):
                m = HN[n] * KC
                kinds = [(0, 0, TC), (1, TC, T)][t0 // TC:]

                def lo(k):
                    ve.wait_ge(hh_ok, m + k + 1)
                    ve.tensor_tensor(hl[:, k, t0:T], n32[:, k % 2, t0:T], hh[:, k, t0:T], ALU.subtract).then_inc(h_ok, 1)

                ve.wait_ge(c_bc, n + 1)
                for k in range(KC):
                    ve.tensor_tensor(nt[:, k % 2, t0:T], x[:, k, t0:T], OB[1][:, t0:T], ALU.mult).then_inc(nt_ok, 1)
                    ve.wait_ge(nt_ok, m + k + 1)
                    if k >= 2:
                        ve.wait_ge(h_ok, m + k - 1)
                    for b, a, e in kinds:
                        i = ve.tensor_scalar(n32[:, k % 2, a:e], nt[:, k % 2, a:e], wsc[:, k, b:b + 1], wsh[:, k, b:b + 1],
                                             ALU.mult, ALU.add)
                    i.then_inc(n32_ok, 1)
                    if k:
                        lo(k - 1)
                lo(KC - 1)

            def residual(k, banks, t0):
                kinds = [(0, 0, TC), (1, TC, T)][t0 // TC:]
                for m in range(2):
                    for b, a, e in kinds:
                        xs = x[:, bass.ds(k + m, 1), a:e]
                        g = gcol[:, :, b]
                        i = ve.scalar_tensor_tensor(xs, banks[m][:, None, a:e], g[:, bass.ds(k + m, 1)], xs, ALU.mult, ALU.add)
                    i.then_inc(xup, 1)

            for s, n in [(lo_done, LO), (conv_ok, 2), (o_free[0], 1), (o_free[1], 1), (y_ok, 1), (a_free, 1), (a32_ok, 2),
                         (al_ok, 2), (qkr_ok, 1), (w_ok, 2), (xup, 4)]:
                ve.sem_inc(s, n)
            ve.memset(eps, EPS).then_inc(eps_ok, 1)
            first = small[:, 44:44 + 4 * ADA_HALF].rearrange("p (u m c) -> p u m c", u=ADA_HALF, m=2)
            ve.wait_ge(srow_ok, 1)
            for n in range(ADA_HALF):
                ve.wait_ge(in_turned[n], 16)
                if n:
                    ve.wait_ge(ada0_sum, n)
                for m in range(2):
                    for c in range(2):
                        i = ve.scalar_tensor_tensor(afdump[:, 2 * m + c, :], aturned[:, n, m, :], 1.0, araw[:, c * D:(c + 1) * D],
                                                    ALU.mult, ALU.mult, accum_out=first[:, n, m, c:c + 1])
                i.then_inc(ada0_sum, 1)
                if n == 1:
                    ve.wait_ge(sqd, 1)
                    ve.tensor_copy(ssq[:, :], sq[:, 0, :]).then_inc(ssd, 1)
                    for k in range(1, KC):
                        add_square(k, 0, k % 2)
                if n == 2:
                    inverse(0, 0)
            ve.wait_ge(ada0_sum, ADA_HALF)
            step(ve.tensor_tensor(adac[:, 0, 8:16, :], first.rearrange("p u m c -> p (u m) c"),
                                  cc("bada", 8, 16)[:, :, None].to_broadcast([P, 8, 2]), ALU.add))
            ve.wait_ge(a0_mm, 1)
            step(ve.tensor_tensor(adac[:, 0, 0:8, :], AB[:, 0:16].rearrange("p (c b) -> p c b", b=2),
                                  cc("bada", 0, 8)[:, :, None].to_broadcast([P, 8, 2]), ALU.add))
            columns(0, cc("n1w", 0, KC), 0)
            ve.wait_ge(dth_ok, 1)
            ve.scalar_tensor_tensor(dtl, dtraw, WS, dth, ALU.mult, ALU.subtract).then_inc(dtl_ok, 1)
            cvt(Unit(U_SSD0), 1024)
            h_lo(0, 0)
            cvt(Unit(U_SSD0 + 1), 1024)
            cvt(Unit(U_SSD0 + 2))

            def conv_tile(g, tile):
                n = g * 6 + tile
                base = g * 36 + tile * 6
                cw = cc("conv")
                ac = acc.rearrange("p (s t) -> p s t", s=2)
                ve.wait_ge(pre_ok, n + 1)
                if not (isinstance(g, int) and tile == 0):
                    ve.wait_ge(xbc_ok, n)
                ve.tensor_scalar(ac, pre[:, tile % 2, :, 0:TC], cw[:, bass.ds(base, 1)], cw[:, bass.ds(base + 5, 1)],
                                 ALU.mult, ALU.add).then_inc(conv, 1)
                for j in range(1, 5):
                    ve.wait_ge(conv, n * 4 + j)
                    ve.scalar_tensor_tensor(ac, pre[:, tile % 2, :, j:j + TC], cw[:, bass.ds(base + j, 1)], ac, ALU.mult,
                                            ALU.add).then_inc(conv if j < 4 else conv_ok, 1)

            ve.wait_ge(dt_mm, 1)
            db = cc("dtb")
            ve.scalar_tensor_tensor(dx.rearrange("p (c h) -> p c h", c=NCH), OB[0][:, 0:256].rearrange("p (c h) -> p c h", c=NCH),
                                    1.0 / (WS * AS), db[:, None, :].to_broadcast([P, NCH, 64]), ALU.mult, ALU.add).then_inc(dtv, 1)
            conv_tile(0, 0)
            ve.wait_ge(dta, 2)
            step(ve.tensor_scalar(dr, de, 2.0, None, ALU.add))
            step(ve.reciprocal(dr, dr))
            step(ve.tensor_tensor(dz, de, dr, ALU.mult))
            step(ve.tensor_tensor(dz2, dz, dz, ALU.mult))
            step(ve.tensor_scalar(dq, dz2, 1.0 / 17.0, None, ALU.mult))
            for k in (15, 13, 11, 9, 7, 5, 3):
                step(ve.scalar_tensor_tensor(dq, dq, 1.0 / k, dz2, ALU.add, ALU.mult))
            step(ve.scalar_tensor_tensor(dq, dq, 1.0, dz, ALU.add, ALU.mult))
            step(ve.tensor_scalar(dr, dx, 0.0, None, ALU.max))
            dtf = PR[:, LDT].rearrange("p c h -> p (c h)")
            step(ve.scalar_tensor_tensor(dtf, dq, 2.0, dr, ALU.mult, ALU.add))
            step(ve.tensor_scalar(dtf, dtf, TINY, None, ALU.max))
            ve.wait_ge(dta, 3)
            step(ve.tensor_scalar(da, da, -DS, None, ALU.mult))
            step(ve.tensor_tensor(dr.rearrange("p (c h) -> p c h", c=NCH), dtf.rearrange("p (c h) -> p c h", c=NCH),
                                  da[:, None, :].to_broadcast([P, NCH, 64]), ALU.mult))
            step(ve.tensor_copy(adh, dr))
            ve.tensor_tensor(adl, dr, adh, ALU.subtract).then_inc(adt_ok, 1)

            def wide(b):
                return b[:, :].rearrange("p (h f) -> p h f", h=HG)

            def per_head(q, c, d):
                a = PRg[:, q, 2 * c + d, :]
                return a[:, :, None].to_broadcast([P, HG, HP])

            def chunk(g, c, between=None):
                if c == 0:
                    ve.wait_ge(o_free[1], g * O_PER + (O_CB[1] + 2))
                for q in range(2):
                    n = g * 8 + (2 * c + q)
                    ve.wait_ge(e_ok, g * 16 + (4 * c + 2 * q + 4))
                    ve.tensor_tensor(E[:, q, 0], E[:, q, 0], E[:, q, 1], ALU.add).then_inc(tsum, 1)
                    ve.wait_ge(tsum, n + 1)
                    ve.tensor_tensor(E[:, q, 0], E[:, q, 0], cb[:, c, None, :].to_broadcast([P, 4, P]), ALU.mult).then_inc(t_ok, 1)
                    if between and q in between:
                        between[q]()
                parts = []
                for d in sorted(YOFF[c]):
                    f = YOFF[c][d][1]
                    dst = (ya, yb)[d]
                    ve.wait_ge(o_mm[d], g * O_PER + (f + 1))
                    ve.tensor_tensor(dst.rearrange("p (h f) -> p h f", h=HG), wide(OB[d]), per_head(DOUT, c, d), ALU.mult).then_inc(o_free[d], 1)
                    ve.wait_ge(o_free[d], g * O_PER + (f + 2))
                    parts.append(dst)
                if len(parts) == 2:
                    ve.tensor_tensor(ya, ya, yb, ALU.add).then_inc(yp, 1)
                    ve.wait_ge(yp, g * 2 + (c - 1))
                ve.wait_ge(yd, g * 8 + (2 * c + 4))
                ve.tensor_tensor(ys[:, c % 2, :], parts[0], YB[:, :], ALU.add).then_inc(y_ok, 1)

            def skip(g, c):
                ve.wait_ge(xD_ok, g * QT + QT)
                ve.wait_ge(a_mm, g * A_PER + (A_YT[c] + 3))
                ve.wait_ge(g_ok, g * NCH + (c + 1))
                ve.tensor_tensor(gt[:, c % 2, :].rearrange("p (q l) -> p q l", q=QT), AB[:, :].rearrange("p (q l) -> p q l", q=QT),
                                 xD[:, :, c * P:(c + 1) * P], ALU.add).then_inc(a_free, 1)

            def group(g, u, more):
                PRf = PR.rearrange("p q c h -> p (q c) h")
                ve.tensor_copy(PRg.rearrange("p q c h -> p (q c) h"), PRf[:, :, bass.ds(g * HG, HG)]).then_inc(prg_ok, 1)
                ve.tensor_copy(adgh.rearrange("p (c h) -> p c h", c=8), adh.rearrange("p (c h) -> p c h", c=8)[:, :, bass.ds(g * HG, HG)]).then_inc(prg_ok, 1)
                ve.tensor_copy(adgl.rearrange("p (c h) -> p c h", c=8), adl.rearrange("p (c h) -> p c h", c=8)[:, :, bass.ds(g * HG, HG)]).then_inc(prg_ok, 1)
                ve.tensor_copy(dg, cc("dskip")[:, bass.ds(g * QT, QT)]).then_inc(prg_ok, 1)
                cvt(u.plus(1))
                ve.wait_ge(prg_ok, g * 4 + 4)
                for c in range(NCH):
                    b, f = O_XT[c]
                    ve.wait_ge(o_mm[b], g * O_PER + (f + 1))
                    ve.tensor_copy(xt[:, c, :], OB[b][:, :]).then_inc(o_free[b], 1)
                cvt(u.plus(2), 1024 if more else UF)
                for k in range(2, 6):
                    b, f = O_ST[k]
                    ve.wait_ge(o_mm[b], g * O_PER + (f + 1))
                    ve.wait_ge(hm_ok, g * 4 + (k - 1))
                    ve.tensor_tensor(Hs[:, k, :], Hs[:, k, :], OB[b][:, :], ALU.add).then_inc(o_free[b], 1)
                if more:
                    cvt(u.plus(3), 1024)
                chunk(g, 0, {1: lambda: cvt(u.plus(4))} if more else None)
                chunk(g, 1, {0: lambda: conv_tile(g + 1, 0), 1: lambda: cvt(u.plus(5))} if more else None)
                skip(g, 0)
                chunk(g, 2, {0: lambda: conv_tile(g + 1, 1), 1: lambda: cvt(u.plus(6))} if more else None)
                skip(g, 1)
                chunk(g, 3, {0: lambda: (conv_tile(g + 1, 2) if more else None, skip(g, 2))})
                if more:
                    conv_tile(g + 1, 3)
                ada_out(g + ADA_FIRST, g * A_PER + A_ADA)
                skip(g, 3)
                if more:
                    conv_tile(g + 1, 4)
                    conv_tile(g + 1, 5)
                else:
                    for q in range(QT):
                        add_square(g * QT + (SQ_G + q), 0, q % 2)

            u = Unit(U_SSD0)
            cvt(u.plus(3))
            conv_tile(0, 1)
            cvt(u.plus(4))
            conv_tile(0, 2)
            conv_tile(0, 3)
            ve.wait_ge(A_mm, 1)
            ve.wait_ge(aexp, 2)
            nega = PR[:, NEGA].rearrange("p c h -> p (c h)")
            ve.wait_ge(ln_ok, 1)
            ve.scalar_tensor_tensor(nega, OB[1][:, 0:256], -1.0 / DS, dtf, ALU.mult, ALU.add).then_inc(pr_ok, 1)
            ve.wait_ge(pr_ok, 1)
            ve.scalar_tensor_tensor(PR[:, DST].rearrange("p c h -> p (c h)"), OB[1][:, 256:512], 1.0 / DS, nega, ALU.mult, ALU.add).then_inc(pr_ok, 1)
            conv_tile(0, 4)
            conv_tile(0, 5)
            ve.wait_ge(aexp, 3)
            with ve.Fori(0, NG - 1) as g:
                group(g, Unit(U_GRP, 6, g), True)
            group(NG - 1, Unit(U_TAIL), False)

            cvt_half(Unit(U_OUT + 1), 0, 0, UF // 2)
            cvt_half(Unit(U_OUT + 1), 1, UF // 2, UF)
            inverse(1, 0)
            gw = small[:, 16:32]
            step(ve.tensor_scalar(gw, cc("gnw"), AS, None, ALU.mult))
            ve.wait_ge(a_free, 1 + 4 * A_PER)
            gates(0, 16, WS * AS)
            step(ve.memset(ssq[:, :], 0.0))
            ve.wait_ge(c_bc, 2)
            for k in range(17):
                if k < 16:
                    if k >= 2:
                        ve.wait_ge(gn_ok, k - 1)
                    ve.scalar_tensor_tensor(nt[:, k % 2, :], G[:, k, :], gw[:, k:k + 1], OB[1][:, :], ALU.mult, ALU.mult).then_inc(gn_t, 1)
                if k:
                    ve.wait_ge(gn_h, k)
                    ve.tensor_tensor(gl[:, k - 1, :], nt[:, (k - 1) % 2, :], gh[:, k - 1, :], ALU.subtract).then_inc(gn_ok, 1)

            def sums(n, t0):
                for m in range(2):
                    add_square(n + m, t0, m)

            with ve.Fori(0, 2) as i:
                for m in range(2):
                    u = Unit(U_OUT + 2 * m, 4, i)
                    cvt_half(u.plus(2), 0, 0, UF // 2)
                    cvt_half(u.plus(2), 1, UF // 2, UF)
                    ada_unit(i * 4 + 2 * m, 0)
                    cvt_half(u.plus(3), 0, 0, UF // 2)
                    ada_unit(i * 4 + (2 * m + 1), 1)
                    ve.wait_ge(unit_done, u.half + (UD + 4))
                    residual(i * 4 + 2 * m, GB[2 * m:2 * m + 2], 0)
                    sums(i * 4 + (SQ_X[2] + 2 * m), 0)
                    cvt_half(u.plus(3), 1, UF // 2, UF)

            def ffn(layer, ugu, udn, t0, with_ada):
                n0 = layer * FC
                cvt_half(Unit(ugu + 2), 0, 0, UF // 2)
                with ve.Fori(0, FC // 2) as i:
                    u = Unit(ugu, 2, i)
                    if with_ada:
                        ada_unit(i * 2 + ADA_OUT, 0)
                    cvt_half(u.plus(2), 1, UF // 2, UF)
                    if with_ada:
                        ada_unit(i * 2 + (ADA_OUT + 1), 1)
                    cvt_half(u.plus(3), 0, 0, UF // 2)
                    ve.wait_ge(unit_done, u.half + (UD + 4))
                    for m in range(2):
                        ve.wait_ge(sg_ok, i * 2 + (n0 + m + 3))
                        ve.wait_ge(al_ok, i * 2 + (n0 + m + 1))
                        ve.scalar_tensor_tensor(a32[:, m, t0:T], GB[2 + m][:, t0:T], FS / (WS * AS), sg[:, m, t0:T], ALU.mult,
                                                ALU.mult).then_inc(a32_ok, 1)
                    cvt_half(u.plus(3), 1, UF // 2, UF)
                    for m in range(2):
                        ve.wait_ge(ah_ok, i * 2 + (n0 + m + 1))
                        am = bass.ds(i * 2 + m, 1)
                        ve.tensor_tensor(al[:, am, t0:T], a32[:, m, None, t0:T], ah[:, am, t0:T], ALU.subtract).then_inc(al_ok, 1)
                    cvt_half(u.plus(4), 0, 0, UF // 2)
                if with_ada:
                    ve.wait_ge(ada_ok, ADA_OUT + ADA_GU)
                gates(layer, 40, WS * FS)
                step(ve.memset(ssq[:, :], 0.0))
                for m in range(4):
                    for k in range(3):
                        if with_ada and m < 3 and k < 2:
                            ada_unit(ADA_OUT + ADA_GU + 2 * m + k, k)
                        nxt = Unit(udn + 3 * m + k + 1)
                        if 0 < 3 * m + k and nxt.base < U_DN1 + 12:
                            a, b = DNK[(k + 1) % 3]
                            cvt_on(nxt, UF if 3 * m + k + 1 == 12 else (b - a) * UN)
                    ve.wait_ge(unit_done, 2 * (udn + 3 * m + 3) + UD)
                    residual(2 * m, GB[2 * (m % 2):2 * (m % 2) + 2], t0)
                    sums(SQ_X[3 + 2 * layer] + 2 * m, t0)

            ve.wait_ge(ada_ok, ADA_OUT)
            columns(0, cc("n2w", 0, KC), 24)
            inverse(2, 0)
            h_lo(2, 0)
            ffn(0, U_GU0, U_DN0, 0, True)

            ve.wait_ge(ada_ok, 48 - ADA_PE)
            columns(1, cc("n1w", KC, 2 * KC), 0)
            gates(1, 16, WS * AS)
            inverse(3, 0)
            h_lo(3, 0)
            lq = cc("lqk").rearrange("p (s a d) -> p s a d", s=2, a=2)
            ve.tensor_tensor(lp, lq[:, 0], lq[:, 1], ALU.mult).then_inc(lam, 1)
            ve.wait_ge(lam, 1)
            ve.tensor_reduce(ls, lp, AXX, ALU.add).then_inc(lam, 1)
            ve.wait_ge(lam, 3)
            ve.scalar_tensor_tensor(nlam, ls[:, 1:2], LAMBDA_INIT, ls[:, 0:1], ALU.subtract, ALU.subtract).then_inc(lam, 1)
            sub = small[:, 8:9]
            step(ve.tensor_scalar(sub, cc("subln"), AS * (1.0 - LAMBDA_INIT), None, ALU.mult))
            step(ve.memset(ssq[:, :], 0.0))
            with ve.Fori(0, 2) as i:
                cvt_on(Unit(U_V + 1, 2, i))
                cvt_on(Unit(U_V + 2, 2, i))

            def turn(i):
                lat = kst[:, :, TC:T]
                for n, (src, b, dst) in enumerate([(qst, AB, qr), (lat, YB, kr[:, :, TC:T])]):
                    ve.wait_ge(rot_mm, i * 2 + (n + 1))
                    ve.tensor_tensor(r1, b[:, :].rearrange("p (h t) -> p h t", h=2), sinT[:, None, :].to_broadcast([P, 2, TC]), ALU.mult).then_inc(rope, 1)
                    ve.tensor_tensor(r2, src, cosT[:, None, :].to_broadcast([P, 2, TC]), ALU.mult).then_inc(rope, 1)
                    ve.wait_ge(rope, i * 6 + (3 * n + 2))
                    ve.tensor_tensor(dst, r1, r2, ALU.add).then_inc(rope, 1)
                    ve.wait_ge(rope, i * 6 + (3 * n + 3))
                ve.tensor_copy(kr[:, :, 0:TC], kst[:, :, 0:TC]).then_inc(qkr_ok, 1)

            def maxima(i, n):
                N = i * 4 + n
                ve.wait_ge(s_mm, N + 1)
                for m in range(2):
                    ve.tensor_reduce(mx[:, n % 2, m:m + 1], SB[n % 2][m][:, :], AXX, ALU.max).then_inc(mx_ok, 1)
                ve.wait_ge(mx_ok, N * 2 + 2)
                ve.tensor_scalar(nb[:, n % 2, :], mx[:, n % 2, :], -0.125, None, ALU.mult).then_inc(nb_ok, 1)

            def weigh(i, n):
                N, b = i * 4 + n, n % 2
                ve.wait_ge(ea_ok, N + 3)
                ve.reciprocal(rs[:, b, :], es[:, b, :]).then_inc(rs_ok, 1)
                ve.wait_ge(rs_ok, N * 2 + 1)
                ve.tensor_scalar(rs[:, b, 1:2], rs[:, b, 1:2], nlam, None, ALU.mult).then_inc(rs_ok, 1)
                ve.wait_ge(rs_ok, N * 2 + 2)
                ve.tensor_scalar(EA[:, b, 1, :], EA[:, b, 1, :], rs[:, b, 1:2], None, ALU.mult).then_inc(w_t, 1)
                ve.wait_ge(w_t, N + 1)
                ve.wait_ge(wt_mm, N + 1)
                ve.scalar_tensor_tensor(wmt[:, b, :], EA[:, b, 0, :], rs[:, b, 0:1], EA[:, b, 1, :], ALU.mult, ALU.add).then_inc(w_ok, 1)

            ve.wait_ge(lam, 4)
            cvt_on(Unit(U_QK + 1))
            cvt_on(Unit(U_QK + 2))
            with ve.Fori(1, 4) as i:
                u = Unit(U_QK, 2, i)
                j = i - 1
                cvt_half(u.plus(1), 1, UF // 2, UF)
                turn(j)
                cvt_half(u.plus(2), 0, 0, UF // 2)
                maxima(j, 0)
                maxima(j, 1)
                weigh(j, 0)
                weigh(j, 1)
                maxima(j, 2)
                cvt_half(u.plus(2), 1, UF // 2, UF)
                maxima(j, 3)
                weigh(j, 2)
                cvt_half(u.plus(3), 0, 0, UF // 2)
                weigh(j, 3)
            turn(3)
            maxima(3, 0)
            maxima(3, 1)
            for n in range(4):
                weigh(3, n)
                if n < 2:
                    maxima(3, n + 2)
            ve.wait_ge(ort_s, 1)
            ve.reciprocal(ort.rearrange("p b h -> p (b h)"), ort.rearrange("p b h -> p (b h)")).then_inc(ort_ok, 1)
            ve.wait_ge(ort_ok, 1)
            for j in range(4):
                hs, b = slice(4 * (j // 2), 4 * (j // 2) + 4), j % 2
                ve.tensor_tensor(osb[:, b, hs], osb[:, b, hs], ort[:, b, hs, None].to_broadcast([P, 4, P]), ALU.mult).then_inc(on_ok, 1)
            for j in range(5):
                if j < 4:
                    ve.wait_ge(ot_mm, j + 1)
                    if j >= 2:
                        ve.wait_ge(o_ok, j - 1)
                    ve.tensor_scalar(o32[:, j % 2, :], OTB[j][:, :], sub, None, ALU.mult).then_inc(o32_ok, 1)
                if j:
                    hq, qb = (j - 1) // 2, (j - 1) % 2
                    ve.wait_ge(oh_ok, j)
                    part = (slice(None), slice(4 * hq, 4 * hq + 4), slice(qb * P, (qb + 1) * P))
                    ve.tensor_tensor(ol[part], o32[:, (j - 1) % 2, :].rearrange("p (h t) -> p h t", h=4), oh[part], ALU.subtract).then_inc(o_ok, 1)
            with ve.Fori(0, 2) as i:
                for m in range(2):
                    cvt_on(Unit(U_WO + m + 1, 2, i))
                    ve.wait_ge(unit_done, i * 4 + (2 * (U_WO + m) + UD + 2))
                    residual(i * 4 + 2 * m, GB[2 * m:2 * m + 2], TC)
                    sums(i * 4 + (SQ_X[4] + 2 * m), TC)
            cvt_half(Unit(U_GU1 + 1), 1, UF // 2, UF)
            columns(1, cc("n2w", KC, 2 * KC), 24)
            inverse(4, 2)
            h_lo(4, TC)
            ffn(1, U_GU1, U_DN1, TC, False)
            inverse(5, 2)
            ve.wait_ge(c_bc, 6)
            fw = cc("fnw")
            for k in range(KC):
                ve.scalar_tensor_tensor(fin[:, k, :], x[:, k, TC:T], fw[:, k:k + 1], OB[1][:, TC:T], ALU.mult, ALU.mult).then_inc(fin_ok, 1)

        @block.gpsimd
        def _(po):
            po.sem_inc(g_ok, 2)
            po.wait_ge(a0_mm, 1)
            po.wait_ge(ada0_sum, ADA_HALF)
            po.memset(pre[:, 0], 0.0).then_inc(pads_ok, 1)
            po.memset(pre[:, 1], 0.0).then_inc(pads_ok, 1)
            po.wait_ge(c_ss, 1)
            po.memset(ssq[:, :], 0.0).then_inc(pads_ok, 1)
            po.wait_ge(pads_ok, 3)

            def group(g, more):
                po.wait_ge(xbc_ok, g * 6 + 6)
                po.wait_ge(prg_ok, g * 4 + 4)

                def summand(k):
                    c, d = ST[k]
                    b, f = O_XT[c]
                    po.wait_ge(o_free[b], g * O_PER + (f + 2))
                    sb_, sf = O_ST[k]
                    if k >= 2:
                        po.wait_ge(o_mm[sb_], g * O_PER + sf)
                    w = PRg[:, DST, 2 * c + d, :]
                    po.tensor_tensor(xdd[:, k % 2, :].rearrange("p (h f) -> p h f", h=HG), xt[:, c, :].rearrange("p (h f) -> p h f", h=HG),
                                     w[:, :, None].to_broadcast([P, HG, HP]), ALU.mult).then_inc(xdd_ok, 1)

                def decay(k):
                    c, d = ST[k]
                    frm = ST_FROM[k]
                    b, f = O_ST[frm]
                    po.wait_ge(o_free[b], g * O_PER + (f + 2))
                    w = PRg[:, DCH, 2 * c + d, :]
                    po.tensor_tensor(Hs[:, k, :].rearrange("p (h f) -> p h f", h=HG), Hs[:, frm, :].rearrange("p (h f) -> p h f", h=HG),
                                     w[:, :, None].to_broadcast([P, HG, HP]), ALU.mult).then_inc(hm_ok, 1)

                summand(0)
                for q in range(QT):
                    po.tensor_scalar(xD[:, q, :], xbc[:, 2 + q, :], dg[:, q:q + 1], 0.0, ALU.mult, ALU.add).then_inc(xD_ok, 1)
                summand(1)
                summand(2)
                summand(3)
                decay(2)
                decay(3)
                summand(4)
                decay(4)
                summand(5)
                decay(5)
                for c in range(NCH):
                    if c == 0:
                        po.wait_ge(zs_ok, g * QT + QT)
                    po.wait_ge(a_free, g * A_PER + (A_YT[c] + 2))
                    gs = G[:, bass.ds(g * QT, QT), c * P:(c + 1) * P]
                    po.tensor_tensor(gs, gs, gt[:, c % 2, :].rearrange("p (q l) -> p q l", q=QT), ALU.mult).then_inc(g_ok, 1)
                if more:
                    for q in range(QT):
                        n = g * QT + (SQ_G + q)
                        po.wait_ge(sqd, n + 1)
                        po.wait_ge(ssd, n)
                        po.tensor_tensor(ssq[:, :], ssq[:, :], sq[:, q % 2, :], ALU.add).then_inc(ssd, 1)

            with po.Fori(0, NG - 1) as g:
                group(g, True)
            group(NG - 1, False)

            po.wait_ge(y_ok, NG * NCH + 1)
            for b in range(2):
                po.dma_start(abuf[:, b], wadaT[ADA_HALF + b]).then_inc(abuf_in[b], 16)
            with po.Fori(0, (48 - ADA_PE) // 2 - 1) as i:
                for b in range(2):
                    po.wait_ge(ada_sum, i * 2 + (b + 1))
                    po.dma_start(abuf[:, b], wadaT[i * 2 + (ADA_HALF + b + 2)]).then_inc(abuf_in[b], 16)

        @block.tensor
        def _(pe):
            def gemm(u, outs, acts, ks, first, last, width=UN, hooks=None, t0=0, t1=T, ready=None):
                ahi, alo = acts
                for j, k in enumerate(ks):
                    if j % 4 == 0:
                        pe.wait_ge(lo_done, u.half + (LO + 1 + j // 4))
                    if ready is not None:
                        pe.wait_ge(ready[0], ready[1] + j + 1)
                    for m, o in outs:
                        wsl = slice(j * width + m * P, j * width + (m + 1) * P)
                        st = k == first
                        en = k == last
                        pe.matmul(o, wh[:, u.slot, wsl], ahi[:, k, t0:t1], start=st, stop=False)
                        pe.matmul(o, wh[:, u.slot, wsl], alo[:, k, t0:t1], start=False, stop=False)
                        i = pe.matmul(o, wl[:, u.slot, wsl], ahi[:, k, t0:t1], start=False, stop=en)
                    if j in (3, len(ks) - 1):
                        i.then_inc(unit_done, 1)
                    if hooks and j in hooks:
                        hooks[j]()

            H = (hh, hl)

            def ssum(n, cs):
                for c in range(cs, 4):
                    i = pe.matmul(OB[0][:, c:c + 1], ssq[:, c * P:(c + 1) * P], ones[:, 0:1], start=True, stop=True)
                i.then_inc(c_ss, 1)

            def bcast(n, cs):
                pe.wait_ge(c_dg, n + 1)
                pe.matmul(OB[1][:, cs * P:T], ones, rdg[:, cs * P:T], start=True, stop=True).then_inc(c_bc, 1)

            def ada(turn, fill):
                pe.wait_ge(araw_in, turn * 16 + 16)
                pe.wait_ge(a_free, fill + 1)
                for m in range(2):
                    for k in range(KC):
                        i = pe.matmul(AB[:, 2 * m:2 * m + 2], araw[:, k * UN + m * P:k * UN + (m + 1) * P], s2[:, k, :],
                                      start=(k == 0), stop=(k == KC - 1))
                i.then_inc(a_mm, 1)

            for s, n in [(unit_done, UD), (yd, 2), (a_mm, 2), (wt_mm, 2)]:
                pe.sem_inc(s, n)
            pe.wait_ge(s2_ok, 1)
            for a in range(ADA_HALF):
                pe.wait_ge(in_ada[a], 16)
                for m in range(2):
                    o = 2 * (2 * a + m)
                    for k in range(KC):
                        i = pe.matmul(AB[:, o:o + 2], afirst[:, a, k * UN + m * P:k * UN + (m + 1) * P], s2[:, k, :],
                                      start=(k == 0), stop=(k == KC - 1))
                if a == 2:
                    pe.wait_ge(in_kp, 16)
                    pe.wait_ge(ssd, KC)
                    ssum(0, 0)
            i.then_inc(a0_mm, 1)
            bcast(0, 0)

            u = Unit(U_SSD0)
            gemm(u, [(0, GB[0][:, :])], H, range(KC), 0, KC - 1, width=P, ready=(h_ok, 0))
            pe.wait_ge(dtl_ok, 1)
            pe.wait_ge(c_rt, 1)
            for c in range(NCH):
                tk = slice(c * P, (c + 1) * P)
                for k in range(KC):
                    o, w_ = OB[0][:, c * 64:(c + 1) * 64], slice(k * 64, (k + 1) * 64)
                    pe.matmul(o, hh[:, k, tk], dth[:, w_], start=(k == 0), stop=False)
                    pe.matmul(o, hl[:, k, tk], dth[:, w_], start=False, stop=False)
                    i = pe.matmul(o, hh[:, k, tk], dtl[:, w_], start=False, stop=(k == KC - 1))
            i.then_inc(dt_mm, 1)
            gemm(u.plus(1), [(0, GB[1][:, :])], H, range(KC), 0, KC - 1, width=P)
            gemm(u.plus(2), [(0, GB[2][:, :]), (1, GB[3][:, :])], H, range(KC), 0, KC - 1)
            pe.wait_ge(masks_ok, 4)
            pe.wait_ge(adt_ok, 1)
            for j, mask in enumerate((masks[:, 0, :], masks[:, 1, :])):
                a8 = slice(32 * j, 32 * j + 32)
                o = OB[1][:, 0:256].rearrange("p (c h) -> p c h", c=NCH)[:, :, a8]
                for n, half in enumerate((adh, adl)):
                    pe.matmul(o, mask, half.rearrange("p (c h) -> p c h", c=NCH)[:, :, a8], start=(n == 0), stop=(n == 1))
            for n, half in enumerate((adh, adl)):
                i = pe.matmul(OB[1][:, 256:512], masks[:, 2, :], half, start=(n == 0), stop=(n == 1))
            i.then_inc(A_mm, 1)
            pe.wait_ge(pre_ok, 2)
            gemm(u.plus(3), [(0, GB[0][:, :]), (1, GB[1][:, :])], H, range(KC), 0, KC - 1)
            pe.wait_ge(dtv, 1)
            pe.wait_ge(aexp, 2)
            pe.wait_ge(pr_ok, 2)

            def group(g, u, more):
                def o_turn(b, f):
                    pe.wait_ge(o_free[b], g * O_PER + (f + 1))

                def x_turn(c):
                    b, f = O_XT[c]
                    if c == 0:
                        pe.wait_ge(xbc_ok, g * 6 + 6)
                    o_turn(b, f)
                    for q in range(QT):
                        i = pe.transpose(OB[b][:, q * P:(q + 1) * P], xbc[:, 2 + q, c * P:(c + 1) * P], ident)
                    i.then_inc(o_mm[b], 1)

                def b_turn():
                    pe.wait_ge(xbc_ok, g * 6 + 2)
                    o_turn(*O_B)
                    for c in range(NCH):
                        i = pe.transpose(OB[0][:, c * P:(c + 1) * P], xbc[:, 0, c * P:(c + 1) * P], ident)
                    i.then_inc(o_mm[0], 1)

                def cb_mm():
                    o_turn(*O_CB)
                    for c in range(NCH):
                        cs = slice(c * P, (c + 1) * P)
                        i = pe.matmul(OB[1][:, cs], xbc[:, 0, cs], xbc[:, 1, cs], start=True, stop=True)
                    i.then_inc(o_mm[1], 1)

                def state(k):
                    c, d = ST[k]
                    b, f = O_ST[k]
                    if k == 0:
                        pe.wait_ge(o_free[0], g * O_PER + (O_B[1] + 2))
                    pe.wait_ge(xdd_ok, g * 6 + (k + 1))
                    o_turn(b, f)
                    pe.matmul(OB[b][:, :], Bt[:, c * P:(c + 1) * P], xdd[:, k % 2, :], start=True, stop=True).then_inc(o_mm[b], 1)

                def exponents(c, q):
                    d, hq = q % 2, q // 2
                    n = g * 16 + (4 * c + q)
                    pe.wait_ge(e_ok, n + 1)
                    if c == 0 and q == 0:
                        pe.wait_ge(prg_ok, g * 4 + 3)
                        pe.wait_ge(zs_ok, g * QT + 2)
                    o = DB[q % 2]
                    pe.matmul(o[:, :].rearrange("p (h l) -> p h l", h=4), idb[:, :], negm[:, d, None, :].to_broadcast([P, 4, P]), start=True, stop=False,
                              skip_group_check=True)
                    for h in range(4):
                        hc = (2 * c + d) * HG + 4 * hq + h
                        for m, half in enumerate((adgh, adgl)):
                            i = pe.matmul(o[:, h * P:(h + 1) * P], half[:, hc:hc + 1].to_broadcast([P, P]), masks[:, d, :],
                                          start=False, stop=(m == 1), skip_group_check=True)
                    i.then_inc(d_mm, 1)

                def within(c, hq):
                    pe.wait_ge(t_ok, g * 8 + (2 * c + hq + 1))
                    if hq == 0:
                        pe.wait_ge(y_ok, g * NCH + (c + 1))
                    for h in range(4):
                        hs = slice((4 * hq + h) * HP, (4 * hq + h + 1) * HP)
                        i = pe.matmul(YB[:, hs], E[:, hq, 0, h, :], xt[:, c, hs], start=(hq == 0 and h == 0), stop=True,
                                      skip_group_check=True)
                    i.then_inc(yd, 1)

                def from_states(c):
                    for d in sorted(YOFF[c]):
                        k, f = YOFF[c][d]
                        sb_, sf = O_ST[k]
                        pe.wait_ge(o_free[sb_], g * O_PER + (sf + 2))
                        if c == 0:
                            pe.wait_ge(bt_ok, g + 1)
                        o_turn(d, f)
                        pe.matmul(OB[d][:, :], Cc[:, c * P:(c + 1) * P], Hs[:, k, :], start=True, stop=True).then_inc(o_mm[d], 1)

                def y_turn(c):
                    pe.wait_ge(y_ok, g * NCH + (c + 2))
                    pe.wait_ge(a_free, g * A_PER + (A_YT[c] + 1))
                    for q in range(QT):
                        i = pe.transpose(AB[:, q * P:(q + 1) * P], ys[:, c % 2, q * P:(q + 1) * P], ident)
                    i.then_inc(a_mm, 1)

                def scan(c):
                    def first():
                        exponents(c, 0)
                        exponents(c, 1)

                    def last_chunk():
                        if c:
                            within(c - 1, 1)

                    def second():
                        from_states(c)
                        exponents(c, 2)

                    def third():
                        within(c, 0)
                        exponents(c, 3)

                    return {0: first, 1: last_chunk, 2: second, 4: third, 6: lambda: y_turn(c - 1) if c else None}

                def unit(k, outs, hooks, width=UN):
                    gemm(u.plus(k), outs, H, range(KC), 0, KC - 1, width=width, hooks=hooks)

                both = [(0, GB[0][:, :]), (1, GB[1][:, :])]
                pe.wait_ge(e_ok, g * 16 + 2)
                pe.wait_ge(pre_ok, g * 6 + 4)
                unit(0, [(0, GB[2][:, :]), (1, GB[3][:, :])],
                     {1: b_turn, 3: cb_mm, 6: lambda: (x_turn(0), x_turn(1)), 7: lambda: (x_turn(2), x_turn(3))})
                pe.wait_ge(pre_ok, g * 6 + 6)
                unit(1, both, {1: lambda: state(0), 2: lambda: state(1), 3: lambda: state(2), 4: lambda: state(3),
                               6: lambda: state(4), 7: lambda: state(5)})
                pe.wait_ge(zs_ok, g * QT + 4)
                for c in range(4):
                    hooks = scan(c)
                    if more:
                        if c < 2:
                            unit(2 + c, [(0, GB[c][:, :])], hooks, P)
                        else:
                            pe.wait_ge(pre_ok, g * 6 + (8 if c == 2 else 10))
                            unit(2 + c, both, hooks)
                    else:
                        for k in sorted(hooks):
                            hooks[k]()
                ada(g, g * A_PER + A_ADA)
                within(3, 1)
                y_turn(3)

            with pe.Fori(0, NG - 1) as g:
                group(g, Unit(U_GRP, 6, g), True)
            group(NG - 1, Unit(U_TAIL), False)

            pe.wait_ge(ssd, SQ_G + 16)
            ssum(1, 0)
            bcast(1, 0)
            with pe.Fori(0, 2) as i:
                for m in range(2):
                    banks = [(j, GB[2 * m + j][:, :]) for j in range(2)]
                    pe.wait_ge(e_ok, 66)
                    pe.wait_ge(xup, i * 4 + (2 * m + 2))
                    for hf in range(2):
                        gemm(Unit(U_OUT + 2 * m + hf, 4, i), banks, (gh, gl), range(8 * hf, 8 * hf + 8), 0, 15,
                             ready=(gn_ok, 8 * hf))

            def ffn(layer, ugu, udn, t0, h0):
                n0 = layer * FC
                with pe.Fori(0, FC // 2) as i:
                    u = Unit(ugu, 2, i)
                    for s in range(2):
                        if s == 0:
                            pe.wait_ge(sg_ok, i * 2 + (n0 + 2))
                        else:
                            pe.wait_ge(a32_ok, i * 2 + (n0 + 2))
                        banks = [(j, GB[2 * s + j][:, t0:T]) for j in range(2)]
                        gemm(u.plus(s), banks, H, range(KC), 0, KC - 1, t0=t0, ready=(h_ok, h0) if s == 0 else None)
                pe.wait_ge(a32_ok, n0 + FC + 2)
                for m in range(4):
                    banks = [(j, GB[2 * (m % 2) + j][:, t0:T]) for j in range(2)]
                    if m >= 2:
                        pe.wait_ge(xup, 12 + 16 * layer + 2 * (m - 1))
                    for k, (a, b) in enumerate(DNK):
                        gemm(Unit(udn + 3 * m + k), banks, (ah, al), range(a, b), 0, FC - 1, t0=t0,
                             ready=(al_ok, 2 + n0 + a) if m == 0 else None)

            def norm(n, cs, sums):
                pe.wait_ge(ssd, sums)
                ssum(n, cs)
                bcast(n, cs)

            norm(2, 0, SQ_X[3])
            ffn(0, U_GU0, U_DN0, 0, KC)

            norm(3, 0, SQ_X[4])
            with pe.Fori(0, 2) as i:
                for s in range(2):
                    u = Unit(U_V + s, 2, i)
                    for k in range(KC):
                        if k % 4 == 0:
                            pe.wait_ge(lo_done, u.half + (LO + 1 + k // 4))
                        if s == 0:
                            pe.wait_ge(h_ok, 2 * KC + k + 1)
                        w_ = slice(k * UN, (k + 1) * UN)
                        for c in range(4):
                            if s == 0 and k == 0:
                                pe.wait_ge(v_ok, i * 4 + (c + 1))
                            o, tk = GB[c][:, s * UN:(s + 1) * UN], slice(c * P, (c + 1) * P)
                            pe.matmul(o, hh[:, k, tk], wh[:, u.slot, w_], start=(k == 0), stop=False)
                            pe.matmul(o, hl[:, k, tk], wh[:, u.slot, w_], start=False, stop=False)
                            j = pe.matmul(o, hh[:, k, tk], wl[:, u.slot, w_], start=False, stop=(k == KC - 1))
                        if k % 4 == 3:
                            j.then_inc(unit_done, 1)

            def scores(i, n):
                hd, qb = n // 2, n % 2
                if n == 0:
                    pe.wait_ge(qkr_ok, i + 2)
                pe.wait_ge(ea_ok, i * 4 + (n + 1))
                for m in range(2):
                    rows = slice(m * HP, (m + 1) * HP)
                    j = pe.matmul(SB[n % 2][m][:, :], qr[rows, hd, qb * P:(qb + 1) * P], kr[rows, hd, :], start=True, stop=True)
                j.then_inc(s_mm, 1)

            def map_turn(i, n):
                pe.wait_ge(w_ok, i * 4 + (n + 3))
                pe.wait_ge(wt_ok, i * 4 + (n + 1))
                for c in range(4):
                    j = pe.transpose(YB[:, c * P:(c + 1) * P], wmt[:, n % 2, c * P:(c + 1) * P], ident)
                j.then_inc(wt_mm, 1)

            def by_v(i, n):
                pe.wait_ge(wt_ok, i * 4 + (n + 2))
                pe.wait_ge(os_ok, i * 4 + (n + 1))
                for c in range(4):
                    j = pe.matmul(AB[:, 0:P], wT[:, n % 2, c * P:(c + 1) * P], v[:, c, bass.ds(i * 256 + (n // 2) * P, P)],
                                  start=(c == 0), stop=(c == 3))
                j.then_inc(pv_mm, 1)

            def rotate(i):
                pe.wait_ge(qk_ok, i * 4 + 5)
                pe.wait_ge(os_ok, i * 4 + 1)
                pe.wait_ge(wt_ok, i * 4 + 1)
                pe.matmul(AB[:, :].rearrange("p (h t) -> p h t", h=2), perm, qst, start=True, stop=True).then_inc(rot_mm, 1)
                pe.matmul(YB[:, :].rearrange("p (h t) -> p h t", h=2), perm, kst[:, :, TC:T], start=True, stop=True).then_inc(rot_mm, 1)

            def q_mm(i, u, hooks=None):
                pe.wait_ge(qk_ok, i * 4 + 1)
                gemm(u, [(j, GB[j][:, 0:TC]) for j in range(2)], H, range(KC), 0, KC - 1, t0=TC, hooks=hooks)

            def k_mm(i, u, hooks=None):
                pe.wait_ge(qk_ok, i * 4 + 3)
                gemm(u, [(j, GB[j][:, :]) for j in range(2)], H, range(KC), 0, KC - 1, hooks=hooks)

            pe.wait_ge(v_ok, 10)
            q_mm(0, Unit(U_QK))
            pe.wait_ge(v_ok, 12)
            k_mm(0, Unit(U_QK + 1))
            with pe.Fori(1, 4) as i:
                u = Unit(U_QK, 2, i)
                j = i - 1
                q_mm(i, u, {0: lambda: rotate(j), 6: lambda: scores(j, 0)})
                scores(j, 1)
                k_mm(i, u.plus(1), {1: lambda: (map_turn(j, 0), scores(j, 2)), 2: lambda: by_v(j, 0),
                                    3: lambda: (map_turn(j, 1), scores(j, 3)), 4: lambda: by_v(j, 1),
                                    5: lambda: map_turn(j, 2), 6: lambda: by_v(j, 2), 7: lambda: map_turn(j, 3)})
                by_v(j, 3)
            rotate(3)
            scores(3, 0)
            scores(3, 1)
            for n in range(4):
                map_turn(3, n)
                if n < 2:
                    scores(3, n + 2)
                by_v(3, n)
            for j in range(4):
                hq, qb = j // 2, j % 2
                pe.wait_ge(on_ok, j + 1)
                for h in range(4):
                    t = pe.transpose(OTB[j][:, h * P:(h + 1) * P], osb[:, qb, 4 * hq + h, :], ident)
                t.then_inc(ot_mm, 1)
            pe.wait_ge(o_ok, 2)
            with pe.Fori(0, 2) as i:
                for m in range(2):
                    pe.wait_ge(xup, i * 4 + (2 * m + 18))
                    gemm(Unit(U_WO + m, 2, i), [(j, GB[2 * m + j][:, TC:T]) for j in range(2)], (oh, ol), range(KC), 0, KC - 1, t0=0, t1=TC,
                         hooks={3: lambda: pe.wait_ge(o_ok, 4)})
            norm(4, 2, SQ_X[5])
            ffn(1, U_GU1, U_DN1, TC, 3 * KC)
            norm(5, 2, SQ_X[5] + KC)


def packed(w, units):
    k = w.shape[0] // P
    return np.ascontiguousarray(w.reshape(k, P, units, UN).transpose(2, 1, 0, 3).reshape(units, P, k * UN))


def constants():
    i = np.arange(P)
    perm = (i[:, None] == (i ^ 32)[None, :]).astype(np.float32)
    pairs, width, grid = 16, TC, 64
    freqs = (1.0 / (np.float32(10000.0) ** (np.arange(pairs, dtype=np.float32) / np.float32(pairs)))).astype(np.float32)
    t = np.arange(width)
    row, colm = (t // grid).astype(np.float32), (t % grid).astype(np.float32)
    ang = np.concatenate([row[:, None] * freqs, colm[:, None] * freqs], axis=1)
    cos, sin = np.cos(ang).T[i % 32], np.sin(ang).T[i % 32]
    sin = np.where((i % 64 < 32)[:, None], -sin, sin)
    keep = np.concatenate([np.eye(P), np.ones((P, P)), perm, cos, sin], axis=1).astype(np.float32)
    fw, bw = i[:, None] <= i[None, :], i[:, None] >= i[None, :]
    stage = np.concatenate([fw, bw, np.where(fw, 0.0, NEG), np.where(bw, 0.0, NEG)], axis=1).astype(np.float32)
    return keep, stage


def kernel(**inputs):
    import concourse.bacc as bacc
    from concourse.bass_utils import run_bass_kernel_spmd

    a = {n: np.asarray(w) for n, w in inputs.items()}

    def chunks(w):
        return w.reshape(-1, P).T

    def rows(w):
        return np.broadcast_to(w.reshape(1, -1), (P, w.size))

    cw, cb = a["ssd_conv_w"][0], a["ssd_conv_b"][0]
    taps = []
    for g in range(NG):
        starts = [DI + g * P, DI + NG * P + g * P] + [g * 512 + q * P for q in range(QT)]
        for s in starts:
            taps += [cw[:, s:s + P].T, cb[s:s + P, None]]
    parts = {
        "n1w": chunks(a["norm1_w"]), "n2w": chunks(a["norm2_w"]), "fnw": chunks(a["final_norm_w"]),
        "bada": chunks(a["b_ada"]), "conv": np.concatenate(taps, axis=1),
        "dskip": chunks(np.repeat(a["ssd_d"][0], HP)), "gnw": chunks(a["ssd_norm_w"][0]), "subln": chunks(a["da_subln_w"][0]),
        "dtb": rows(a["ssd_dt_bias"][0]), "alog": rows(a["ssd_a_log"][0]),
        "lqk": rows(np.concatenate([a["da_lq1"][0], a["da_lq2"][0], a["da_lk1"][0], a["da_lk2"][0]])),
        "cvec": np.stack([chunks(a["c_ctx"]), chunks(a["c"][0])], axis=2).reshape(P, 2 * KC),
    }
    cols = np.concatenate([parts[n] for n, _ in _sizes], axis=1)
    assert cols.shape == (P, NCOL)
    keep, stage = constants()
    tok = np.concatenate([a["ctx"][0], a["x"][0]], axis=0)
    xT = tok.T.reshape(KC, P, T).transpose(1, 0, 2)

    w_in = a["ssd_w_in"][0]
    def in_cols(s, n):
        return w_in[:, s:s + n].reshape(KC, P, n).transpose(1, 0, 2).reshape(P, KC * n)

    B0, C0, DT0 = 2 * DI, 2 * DI + NG * P, 2 * DI + 2 * NG * P
    wxg = np.stack([np.concatenate([in_cols(B0 + g * P, P), in_cols(C0 + g * P, P), in_cols(DI + g * 512, UN),
                                    in_cols(DI + g * 512 + UN, UN)], axis=1) for g in range(NG)])
    wout = a["ssd_w_out"][0]
    wout = np.stack([packed(wout[h * D:(h + 1) * D], 4) for h in range(2)], axis=1).reshape(8, P, UF)
    gate, up = a["ffn_w_gate"], a["ffn_w_up"]
    wgu = np.concatenate([np.stack([packed(gate[l], FC // 2), packed(up[l], FC // 2)], axis=1).reshape(FC, P, UF) for l in range(2)])
    wdn = np.concatenate([packed(a["ffn_w_down"][l], 4) for l in range(2)])
    wq, wk, wv = [packed(a["da_w_qkv"][0][:, i * D:(i + 1) * D], 4) for i in range(3)]
    data = {
        "cols": cols, "keep": keep, "stage": stage, "xT": xT,
        "wada": packed(a["w_ada"][0], 24)[[*range(ADA_HALF), *range(ADA_FIRST, ADA_PE)]],
        "wadaT": np.concatenate([w.T.reshape(24, 2, P, D).transpose(0, 2, 1, 3) for w in a["w_ada"]])[
            [*range(ADA_HALF, ADA_FIRST), *range(ADA_PE, 48)]],
        "crow": rows(np.concatenate([a["c_ctx"], a["c"][0]])),
        "wdt": in_cols(DT0, 64), "wxg": wxg, "wz": packed(w_in[:, 0:DI], 8), "wout": wout, "wgu": wgu, "wdn": wdn,
        "wv": wv, "wqk": np.stack([wq, wk], axis=1).reshape(8, P, UF), "wo": packed(a["da_w_o"][0], 4),
    }
    data = {n: np.ascontiguousarray(w) for n, w in data.items()}

    nc = bacc.Bacc("TRN2", target_bir_lowering=False, num_devices=1)
    t = {n: nc.dram_tensor(n, list(w.shape), F32, kind="ExternalInput") for n, w in data.items()}
    out = nc.dram_tensor("out", [P, KC, TC], F32, kind="ExternalOutput")
    build(nc, *[t[n].ap() for n in data], out.ap())
    nc.compile()
    y = run_bass_kernel_spmd(nc, [data], core_ids=[0]).results[0]["out"]
    return np.asarray(y).reshape(P, KC, TC).transpose(2, 1, 0).reshape(1, TC, D)
```
